# Optimizing a Trainium2 kernel written in Bass

```python
import math
import jax, jax.numpy as jnp
from jax import lax
import numpy as np

D_MODEL = 1024
BATCH = 1
SEQ = 512
DEPTH = 1

HEAD_DIM = 64
D_MIX = D_MODEL
N_FOX = (3 * D_MIX // 8) // HEAD_DIM
N_MOBA = (3 * D_MIX // 8) // HEAD_DIM
D_FOX = N_FOX * HEAD_DIM
D_MOBA = N_MOBA * HEAD_DIM
D_LRU = D_MIX - D_FOX - D_MOBA
LRU_GROUP = HEAD_DIM
N_LRU_GROUPS = D_LRU // LRU_GROUP
N_OUT_HEADS = D_MIX // HEAD_DIM
Q_BLOCK = 128
MOBA_BLOCK = 256
MOBA_TOPK = 3
MOBA_Q_CHUNK = 64
CONV_WIDTH = 4
LRU_C = 8.0
D_FF = -(-8 * D_MODEL // (3 * 256)) * 256
ALPHA = (2 * DEPTH) ** 0.25
BETA = (8 * DEPTH) ** -0.25
LN_EPS = 1e-5
RMS_EPS = 1e-6
NEG = -1e30
IN_SIZES = [D_FOX, D_FOX, D_FOX, N_FOX,
            D_MOBA, D_MOBA, D_MOBA,
            D_LRU, D_LRU]
N_IN = sum(IN_SIZES)
IN_SPLITS = [int(s) for s in np.cumsum(IN_SIZES)[:-1]]

kernel_name = "hymba_fox_moba_rglru_deepnorm"

def layer_norm(x, g, b):
    xf = x.astype(jnp.float32)
    mu = jnp.mean(xf, axis=-1, keepdims=True)
    var = jnp.mean(jnp.square(xf - mu), axis=-1, keepdims=True)
    y = (xf - mu) * lax.rsqrt(var + LN_EPS)
    return (y * g.astype(jnp.float32) + b.astype(jnp.float32)).astype(x.dtype)

def fox_attention(q, k, v, log_f):
    B, S, H, dh = q.shape
    scale = 1.0 / math.sqrt(dh)
    F = jnp.cumsum(log_f, axis=1).transpose(0, 2, 1)
    nblk = S // Q_BLOCK
    qb = q.reshape(B, nblk, Q_BLOCK, H, dh).transpose(1, 0, 2, 3, 4)
    Fb = F.reshape(B, H, nblk, Q_BLOCK).transpose(2, 0, 1, 3)
    kpos = jnp.arange(S)

    def one_block(args):
        i, q_i, F_i = args
        s = jnp.einsum('bqhd,bkhd->bhqk', q_i, k).astype(jnp.float32) * scale
        s = s + F_i[..., :, None] - F[:, :, None, :]
        qpos = i * Q_BLOCK + jnp.arange(Q_BLOCK)
        causal = kpos[None, :] <= qpos[:, None]
        s = jnp.where(causal, s, NEG)
        p = jax.nn.softmax(s, axis=-1).astype(v.dtype)
        return jnp.einsum('bhqk,bkhd->bqhd', p, v)

    out = lax.map(one_block, (jnp.arange(nblk), qb, Fb))
    return out.transpose(1, 0, 2, 3, 4).reshape(B, S, H * dh)

def moba_attention(q, k, v):
    B, S, H, dh = q.shape
    scale = 1.0 / math.sqrt(dh)
    nb = max(-(-S // MOBA_BLOCK), MOBA_TOPK)
    pad = nb * MOBA_BLOCK - S
    kp = jnp.pad(k, ((0, 0), (0, pad), (0, 0), (0, 0)))
    vp = jnp.pad(v, ((0, 0), (0, pad), (0, 0), (0, 0)))
    kblk = kp.reshape(B, nb, MOBA_BLOCK, H, dh)
    vblk = vp.reshape(B, nb, MOBA_BLOCK, H, dh)
    kmean = jnp.mean(kblk.astype(jnp.float32), axis=2).astype(k.dtype)
    nq = S // MOBA_Q_CHUNK
    qc = q.reshape(B, nq, MOBA_Q_CHUNK, H, dh).transpose(1, 0, 2, 3, 4)
    bi = jnp.arange(B)[:, None, None, None]
    hi = jnp.arange(H)[None, None, :, None]
    blk_ids = jnp.arange(nb)
    own_off = jnp.arange(MOBA_BLOCK)

    def one_chunk(args):
        c, q_c = args
        start = c * MOBA_Q_CHUNK
        cur = start // MOBA_BLOCK
        qpos = start + jnp.arange(MOBA_Q_CHUNK)
        g = jnp.einsum('bqhd,bnhd->bqhn', q_c, kmean).astype(jnp.float32)
        g = jnp.where(blk_ids < cur, g, NEG)
        _, idx = lax.top_k(g, MOBA_TOPK)
        valid = idx < cur
        gk = kblk[bi, idx, :, hi]
        gv = vblk[bi, idx, :, hi]
        s_sel = jnp.einsum('bqhd,bqhnkd->bqhnk', q_c, gk).astype(jnp.float32) * scale
        s_sel = jnp.where(valid[..., None], s_sel, NEG)
        s_sel = s_sel.reshape(B, MOBA_Q_CHUNK, H, MOBA_TOPK * MOBA_BLOCK)
        k_own = lax.dynamic_slice_in_dim(kp, cur * MOBA_BLOCK, MOBA_BLOCK, axis=1)
        v_own = lax.dynamic_slice_in_dim(vp, cur * MOBA_BLOCK, MOBA_BLOCK, axis=1)
        s_own = jnp.einsum('bqhd,bkhd->bqhk', q_c, k_own).astype(jnp.float32) * scale
        kpos_own = cur * MOBA_BLOCK + own_off
        causal = kpos_own[None, :] <= qpos[:, None]
        s_own = jnp.where(causal[None, :, None, :], s_own, NEG)
        p = jax.nn.softmax(jnp.concatenate([s_sel, s_own], axis=-1), axis=-1).astype(v.dtype)
        p_sel = p[..., :MOBA_TOPK * MOBA_BLOCK].reshape(B, MOBA_Q_CHUNK, H, MOBA_TOPK, MOBA_BLOCK)
        p_own = p[..., MOBA_TOPK * MOBA_BLOCK:]
        return (jnp.einsum('bqhnk,bqhnkd->bqhd', p_sel, gv)
                + jnp.einsum('bqhk,bkhd->bqhd', p_own, v_own))

    out = lax.map(one_chunk, (jnp.arange(nq), qc))
    return out.transpose(1, 0, 2, 3, 4).reshape(B, S, H * dh)

def rglru_branch(xb, conv_w, conv_b, w_r, b_r, w_i, b_i, lam):
    B, S, _ = xb.shape
    xp = jnp.pad(xb, ((0, 0), (CONV_WIDTH - 1, 0), (0, 0)))
    xc = conv_b + sum(xp[:, j:j + S] * conv_w[j] for j in range(CONV_WIDTH))
    xg = xc.reshape(B, S, N_LRU_GROUPS, LRU_GROUP)
    r = jax.nn.sigmoid(jnp.einsum('bsgi,gij->bsgj', xg, w_r).reshape(B, S, D_LRU) + b_r)
    i = jax.nn.sigmoid(jnp.einsum('bsgi,gij->bsgj', xg, w_i).reshape(B, S, D_LRU) + b_i)
    log_a = LRU_C * r.astype(jnp.float32) * jax.nn.log_sigmoid(lam.astype(jnp.float32))
    a = jnp.exp(log_a)
    u = jnp.sqrt(-jnp.expm1(2.0 * log_a)) * (i * xc).astype(jnp.float32)

    def combine(e1, e2):
        a1, b1 = e1
        a2, b2 = e2
        return a1 * a2, a2 * b1 + b2

    _, h = lax.associative_scan(combine, (a, u), axis=1)
    return h.astype(xb.dtype)

def headwise_rmsnorm(y, g):
    B, S, _ = y.shape
    yf = y.astype(jnp.float32).reshape(B, S, N_OUT_HEADS, HEAD_DIM)
    yf = yf * lax.rsqrt(jnp.mean(jnp.square(yf), axis=-1, keepdims=True) + RMS_EPS)
    return (yf.reshape(B, S, D_MIX) * g.astype(jnp.float32)).astype(y.dtype)

def setup_inputs(seed: int = 0) -> dict:
    key = jax.random.key(seed)
    ks = jax.random.split(key, 24)
    L = DEPTH
    nrm = jax.random.normal
    x = nrm(ks[0], (BATCH, SEQ, D_MODEL), jnp.float32)
    col_scale = jnp.concatenate([
        jnp.ones((3 * D_FOX,), jnp.float32),
        jnp.full((N_FOX,), 0.1, jnp.float32),
        jnp.ones((3 * D_MOBA + 2 * D_LRU,), jnp.float32)])
    w_in = nrm(ks[1], (L, D_MODEL, N_IN), jnp.float32) * (D_MODEL ** -0.5) * col_scale
    b_fgate = jax.random.uniform(ks[2], (L, N_FOX), jnp.float32, 1.0, 6.0)
    conv_w = nrm(ks[3], (L, CONV_WIDTH, D_LRU), jnp.float32) * (CONV_WIDTH ** -0.5)
    conv_b = 0.01 * nrm(ks[4], (L, D_LRU), jnp.float32)
    w_rgate = nrm(ks[5], (L, N_LRU_GROUPS, LRU_GROUP, LRU_GROUP), jnp.float32) * (LRU_GROUP ** -0.5)
    b_rgate = 0.01 * nrm(ks[6], (L, D_LRU), jnp.float32)
    w_igate = nrm(ks[7], (L, N_LRU_GROUPS, LRU_GROUP, LRU_GROUP), jnp.float32) * (LRU_GROUP ** -0.5)
    b_igate = 0.01 * nrm(ks[8], (L, D_LRU), jnp.float32)
    a8 = jax.random.uniform(ks[9], (L, D_LRU), jnp.float32, 0.9, 0.999)
    p = a8 ** (1.0 / LRU_C)
    lru_lambda = jnp.log(p) - jnp.log1p(-p)
    out_norm_g = 1.0 + 0.02 * nrm(ks[10], (L, D_MIX), jnp.float32)
    w_out = nrm(ks[11], (L, D_MIX, D_MODEL), jnp.float32) * (D_MIX ** -0.5) * BETA
    ln1_g = 1.0 + 0.02 * nrm(ks[12], (L, D_MODEL), jnp.float32)
    ln1_b = 0.01 * nrm(ks[13], (L, D_MODEL), jnp.float32)
    w_ffn_gate = nrm(ks[14], (L, D_MODEL, D_FF), jnp.float32) * (D_MODEL ** -0.5)
    w_ffn_up = nrm(ks[15], (L, D_MODEL, D_FF), jnp.float32) * (D_MODEL ** -0.5)
    w_ffn_down = nrm(ks[16], (L, D_FF, D_MODEL), jnp.float32) * (D_FF ** -0.5) * BETA
    ln2_g = 1.0 + 0.02 * nrm(ks[17], (L, D_MODEL), jnp.float32)
    ln2_b = 0.01 * nrm(ks[18], (L, D_MODEL), jnp.float32)
    return {'x': x, 'w_in': w_in, 'b_fgate': b_fgate, 'conv_w': conv_w, 'conv_b': conv_b,
            'w_rgate': w_rgate, 'b_rgate': b_rgate, 'w_igate': w_igate, 'b_igate': b_igate,
            'lru_lambda': lru_lambda, 'out_norm_g': out_norm_g, 'w_out': w_out,
            'ln1_g': ln1_g, 'ln1_b': ln1_b, 'w_ffn_gate': w_ffn_gate, 'w_ffn_up': w_ffn_up,
            'w_ffn_down': w_ffn_down, 'ln2_g': ln2_g, 'ln2_b': ln2_b}

def reference(x, w_in, b_fgate, conv_w, conv_b, w_rgate, b_rgate, w_igate, b_igate,
              lru_lambda, out_norm_g, w_out, ln1_g, ln1_b, w_ffn_gate, w_ffn_up,
              w_ffn_down, ln2_g, ln2_b):
    B, S, _ = x.shape
    for l in range(DEPTH):
        proj = jnp.einsum('bsd,dn->bsn', x, w_in[l])
        fq, fk, fv, ff, mq, mk, mv, lx, lg = jnp.split(proj, IN_SPLITS, axis=-1)
        heads = lambda t, h: t.reshape(B, S, h, HEAD_DIM)
        log_f = jax.nn.log_sigmoid((ff + b_fgate[l]).astype(jnp.float32))
        y_fox = fox_attention(heads(fq, N_FOX), heads(fk, N_FOX), heads(fv, N_FOX), log_f)
        y_moba = moba_attention(heads(mq, N_MOBA), heads(mk, N_MOBA), heads(mv, N_MOBA))
        h_lru = rglru_branch(lx, conv_w[l], conv_b[l], w_rgate[l], b_rgate[l],
                             w_igate[l], b_igate[l], lru_lambda[l])
        y_lru = jax.nn.gelu(lg) * h_lru
        y = jnp.concatenate([y_fox, y_moba, y_lru], axis=-1)
        y = headwise_rmsnorm(y, out_norm_g[l])
        mix = jnp.einsum('bsm,md->bsd', y, w_out[l])
        x = layer_norm(ALPHA * x + mix, ln1_g[l], ln1_b[l])
        hid = jax.nn.silu(jnp.einsum('bsd,df->bsf', x, w_ffn_gate[l])) * jnp.einsum('bsd,df->bsf', x, w_ffn_up[l])
        ffn = jnp.einsum('bsf,fd->bsd', hid, w_ffn_down[l])
        x = layer_norm(ALPHA * x + ffn, ln2_g[l], ln2_b[l])
    return x


_drawn_inputs = setup_inputs


def setup_inputs(seed=0):
    import zlib

    import numpy as np

    out = dict(_drawn_inputs(seed))
    spreads = {}
    factors = {'conv_b': 2.902,
     'b_rgate': 35.793,
     'b_igate': 28.93,
     'out_norm_g': 6.306,
     'ln1_g': 2.781,
     'ln1_b': 5.269,
     'ln2_g': 8.261,
     'ln2_b': 16.662}
    for name, (base, spread) in spreads.items():
        noise = np.random.default_rng([zlib.crc32(name.encode()), seed]).standard_normal(out[name].shape)
        drawn = base * np.exp(spread * noise) if base else spread * noise
        out[name] = __import__('jax').numpy.asarray(drawn.astype(out[name].dtype))
    for name, factor in factors.items():
        out[name] = (out[name] * factor).astype(out[name].dtype)
    return out
```

```python
import math
from contextlib import ExitStack

import concourse.bass as bass
from concourse import mybir



def hymba_layer(nc, x, w_in, b_fgate, conv_w, conv_b, w_rgate, b_rgate, w_igate, b_igate, lru_lambda,
                out_norm_g, w_out, ln1_g, ln1_b, w_ffn_gate, w_ffn_up, w_ffn_down, ln2_g, ln2_b, out):
    F32 = mybir.dt.float32
    F32R = mybir.dt.float32r
    ALU = mybir.AluOpType
    ACT = mybir.ActivationFunctionType

    P = 128
    _, S, D = x.shape
    DC = D // P
    ST = S // P
    NFOX = b_fgate.shape[1]
    DH = w_rgate.shape[2]
    DLRU = conv_b.shape[1]
    DFOX = NFOX * DH
    DMOBA = D - DLRU - DFOX
    F = w_ffn_gate.shape[2]
    FT = F // P
    CW = conv_w.shape[1]
    H2 = S
    PAIRS = (DFOX + DMOBA) // P
    FOXP = DFOX // P
    MOBAP = DMOBA // P
    LT = DLRU // P
    YT = D // P
    ALPHA = 2 ** 0.25
    SCALE = 1.0 / math.sqrt(DH)
    BIG = 1e30
    LRU_C = 8.0
    LN_EPS = 1e-5
    RMS_EPS = 1e-6
    BN = 512

    C_FQ, C_FK, C_FV, C_FF = 0, DFOX, 2 * DFOX, 3 * DFOX
    C_MQ = C_FF + NFOX
    C_MK = C_MQ + DMOBA
    C_MV = C_MK + DMOBA
    C_LX = C_MV + DMOBA
    C_LG = C_LX + DLRU

    U_FF = 2 * LT
    U_QKV = U_FF + 1
    U_OUT = U_QKV + 3 * PAIRS
    U_FFN = U_OUT + YT
    U_DOWN = U_FFN + 2 * FT
    SLOTS = 4
    proj_col = [C_LX + P * t for t in range(LT)] + [C_LG + P * t for t in range(LT)] + [C_FF]
    for p in range(MOBAP):
        proj_col += [C_MQ + P * p, C_MK + P * p, C_MV + P * p]
    for p in range(FOXP):
        proj_col += [C_FQ + P * p, C_FK + P * p, C_FV + P * p]
    y_tile = [FOXP + MOBAP + t for t in range(LT)]
    y_tile += [FOXP + p for p in range(MOBAP)] + [p for p in range(FOXP)]
    NORMS = YT
    out_tiles = list(y_tile)

    assert max(-(-S // 256), 3) == 3

    ctx = ExitStack()
    common = ctx.enter_context(ExitStack())

    def sb(stack, name, shape, dt=F32):
        return stack.enter_context(nc.sbuf_tensor(name, shape, dt))

    def sem(name):
        return ctx.enter_context(nc.semaphore(name))

    raw = sb(common, "raw", [P, SLOTS, D])
    w_hi = sb(common, "w_hi", [P, SLOTS, D], F32R)
    w_lo = sb(common, "w_lo", [P, SLOTS, D], F32R)
    a_hi = sb(common, "a_hi", [P, DC, S], F32R)
    a_lo = sb(common, "a_lo", [P, DC, S], F32R)
    x_nat = sb(common, "x_nat", [P, ST, D])
    gb = sb(common, "gb", [P, 2, D])
    ident = sb(common, "ident", [P, P])
    stats = sb(common, "stats", [P, 2, D // BN, 6])
    mv = sb(common, "mv", [P, 2, 2])
    eps = sb(common, "eps", [P, 2])
    rstd_ln = sb(common, "rstd_ln", [P, 2])

    mix = ExitStack()
    q_hi = sb(mix, "q_hi", [P, 2, S], F32R)
    q_lo = sb(mix, "q_lo", [P, 2, S], F32R)
    k_hi = sb(mix, "k_hi", [P, 2, S], F32R)
    k_lo = sb(mix, "k_lo", [P, 2, S], F32R)
    vT = sb(mix, "vT", [P, S])
    vv = sb(mix, "vv", [P, ST, 2, 2 * DH], F32R)
    yraw = sb(mix, "yraw", [P, 2, S])
    otmp = sb(mix, "otmp", [DH, S])
    sq = sb(mix, "sq", [P, S])
    rstd = sb(mix, "rstd", [P, S])
    yn = sb(mix, "yn", [P, YT, S])
    mask = sb(mix, "mask", [P, S])
    blockmean = sb(mix, "blockmean", [P, P])
    gate_w = sb(mix, "gate_w", [P, 2 * LT, P])
    par_rows = sb(mix, "par_rows", [P, P])
    par = sb(mix, "par", [P, 32])
    lam = sb(mix, "lam", [P, 8, LT])
    fox_q = sb(mix, "fox_q", [P, 2, S], F32R)
    fox_g = sb(mix, "fox_g", [P, S], F32R)
    fox_k = sb(mix, "fox_k", [P, S], F32R)
    onehot = sb(mix, "onehot", [P, NFOX])
    bf = sb(mix, "bf", [NFOX, 1])
    nmax = sb(mix, "nmax", [P, 2])
    rsum = sb(mix, "rsum", [P, 2])
    rinv = sb(mix, "rinv", [P, 2])

    lru = ExitStack()
    xb = sb(lru, "xb", [P, LT, CW - 1 + S])
    ri = sb(lru, "ri", [P, 2, LT, S])
    xc = sb(lru, "xc", [P, LT, S])
    a_t = sb(lru, "a_t", [P, LT, S])
    th = sb(lru, "th", [P, LT, S])
    lg = sb(lru, "lg", [P, LT, S])
    lru.close()
    att = ExitStack()
    PT_STRIDE = S - P
    PT_COLS = (ST - 1) * PT_STRIDE + S
    pt_hi = sb(att, "pt_hi", [P, 2, PT_COLS], F32R)
    pt_lo = sb(att, "pt_lo", [P, 2, PT_COLS], F32R)
    smask = sb(att, "smask", [P, 2, S])
    prob = sb(att, "prob", [P, 2, S])
    att.close()
    mix.close()

    ffn = ExitStack()
    hid = sb(ffn, "hid", [P, FT * S])
    h_hi = sb(ffn, "h_hi", [P, SLOTS, S], F32R)
    h_lo = sb(ffn, "h_lo", [P, SLOTS, S], F32R)
    silu = sb(ffn, "silu", [P, 2, S])
    z = sb(ffn, "z", [P, 2, D])
    ffn.close()

    fg = yn[0:NFOX, 2:YT, :]

    psum = ctx.enter_context(nc.psum_tensor("psum", [P, 8, H2], F32))
    B_SCORE, B_TRANS, B_OUT = 2, 4, 6

    x_in = [sem(f"x_in{g}") for g in range(ST)]
    raw_in = [sem(f"raw_in{i}") for i in range(SLOTS)]
    par_in = sem("par_in")
    gate_in = sem("gate_in")
    gb_in = sem("gb_in")
    pad_made = sem("pad_made")
    ident_made = sem("ident_made")
    consts_made = sem("consts_made")
    pool_step = sem("pool_step")
    x_tr = sem("x_tr")
    x_hi_done = sem("x_hi_done")
    x_lo_done = sem("x_lo_done")
    w_hi_done = sem("w_hi_done")
    w_lo_done = sem("w_lo_done")
    unit_used = sem("unit_used")
    par_tr = sem("par_tr")
    par_done = sem("par_done")
    xb_done = sem("xb_done")
    conv_done = sem("conv_done")
    gates_mm = sem("gates_mm")
    gates_done = sem("gates_done")
    gelu_done = sem("gelu_done")
    decay_done = sem("decay_done")
    logexp_done = sem("logexp_done")
    log_decay_done = sem("log_decay_done")
    ff_read = sem("ff_read")
    fox_ready = sem("fox_ready")
    fox_q_done = sem("fox_q_done")
    lru_done = sem("lru_done")
    sq_done = sem("sq_done")
    ms_mm = sem("ms_mm")
    ms_read = sem("ms_read")
    yn_done = sem("yn_done")
    q_hi_done = sem("q_hi_done")
    k_hi_done = sem("k_hi_done")
    q_lo_done = sem("q_lo_done")
    k_lo_done = sem("k_lo_done")
    vT_done = sem("vT_done")
    v_tr = sem("v_tr")
    v_hi_done = sem("v_hi_done")
    v_lo_done = sem("v_lo_done")
    scores = sem("scores")
    masked = sem("masked")
    exps = sem("exps")
    probs = sem("probs")
    p_tr = sem("p_tr")
    pt_hi_done = sem("pt_hi_done")
    pt_lo_done = sem("pt_lo_done")
    pv_done = sem("pv_done")
    o_copied = sem("o_copied")
    half_added = sem("half_added")
    y_hi_done = sem("y_hi_done")
    y_lo_done = sem("y_lo_done")
    rows_mixed = sem("rows_mixed")
    sum_done = sem("sum_done")
    x1_done = sem("x1_done")
    x1_tr = sem("x1_tr")
    x1_hi_done = sem("x1_hi_done")
    x1_lo_done = sem("x1_lo_done")
    silu_done = sem("silu_done")
    hid_done = sem("hid_done")
    h_hi_done = sem("h_hi_done")
    h_lo_done = sem("h_lo_done")
    root_arg = sem("root_arg")
    root_done = sem("root_done")
    rstd_done = sem("rstd_done")
    var_done = sem("var_done")
    var_log = sem("var_log")
    rstd_ln_done = sem("rstd_ln_done")
    out_ready = sem("out_ready")
    out_stored = [sem("out_stored0"), sem("out_stored1")]
    rows_down = sem("rows_down")
    dve_step = sem("dve_step")

    w_in_v = w_in[0].rearrange("(c p) n -> p c n", p=P)
    gate_v = w_ffn_gate[0].rearrange("(c p) n -> p c n", p=P)
    up_v = w_ffn_up[0].rearrange("(c p) n -> p c n", p=P)
    x_v = x[0].rearrange("(t p) d -> p t d", p=P)
    out_v = out[0].rearrange("(t p) d -> p t d", p=P)

    def f32(ap):
        return ap.bitcast(F32)

    def unit(u):
        return u % SLOTS

    def score_no(p, i, h):
        return (p * ST + i) * 2 + h + 1

    def by_key(buf, h, i):
        row = buf[:, h, i * P:(i + 1) * P]
        return bass.AP(row.tensor, row.offset, [row.ap[0], [PT_STRIDE, i + 1], [1, P]])

    def blocks(bank, n):
        return psum[:, bank, 0:n * P].rearrange("p (j c) -> p j c", c=P)

    def heads(part):
        return vv[:, :, :, part * DH:(part + 1) * DH]

    def v_blocks():
        return psum[:, B_TRANS, :].rearrange("p (t h c) -> p t h c", t=ST, h=2)

    def wait_y(eng, n):
        if n < LT:
            eng.wait_ge(lru_done, n + 1)
        else:
            eng.wait_ge(half_added, 2 * (n - LT) + 2)

    R_CONV, R_CONVB, R_BR = 0, CW * LT, (CW + 1) * LT
    R_BI, R_LAM, R_G = R_BR + LT, R_BR + 2 * LT, R_BR + 3 * LT
    NPAR = R_G + YT
    PAR_DMAS = 7
    DOWN_TURNS = (FT - 6) // 4

    ATANH = [1.0 / (2 * n + 1) for n in range(1, 9)]

    block = ctx.enter_context(nc.Block())

    @block.sync
    def _(sp):
        def load(u, dst, src):
            if u >= SLOTS:
                sp.wait_ge(w_lo_done, u - SLOTS + 1)
            sp.dma_start(dst, src).then_inc(raw_in[unit(u)], 16)

        def by_chunk(u):
            return raw[:, unit(u), :].rearrange("p (c n) -> p c n", c=DC)

        W = D // ST
        for g in range(ST):
            sp.dma_start(x_nat[:, :, g * W:(g + 1) * W], x_v[:, :, g * W:(g + 1) * W]).then_inc(x_in[g], 16)
            if g == 0:
                load(0, by_chunk(0), w_in_v[:, :, proj_col[0]:proj_col[0] + P])
        for u in range(1, U_OUT):
            load(u, by_chunk(u), w_in_v[:, :, proj_col[u]:proj_col[u] + P])
        for n, m in enumerate(out_tiles):
            load(U_OUT + n, raw[:, unit(U_OUT + n), :], w_out[0, m * P:(m + 1) * P, :])
        with sp.Fori(0, FT // 2) as it:
            for k in range(4):
                u = U_FFN + k
                sp.wait_ge(w_lo_done, it * 4 + (u - SLOTS + 1))
                sp.dma_start(by_chunk(u), (gate_v, up_v)[k % 2][:, :, bass.ds(it * (2 * P) + (k // 2) * P, P)])\
                  .then_inc(raw_in[unit(u)], 16)
        for i, v in enumerate((ln2_g, ln2_b)):
            sp.wait_ge(x1_done, ST)
            sp.dma_start(gb[:, i, :], v[0].partition_broadcast(P)).then_inc(gb_in, 16)
        for f in range(FT):
            load(U_DOWN + f, raw[:, unit(U_DOWN + f), :], w_ffn_down[0, f * P:(f + 1) * P, :])
        for s in range(ST):
            sp.wait_ge(out_ready, s + 1)
            sp.dma_start(out_v[:, s, :], z[:, s % 2, :]).then_inc(out_stored[s % 2], 16)
        for b in range(2):
            sp.wait_ge(out_stored[b], 16 * (ST // 2))

    @block.gpsimd
    def _(pool):
        steps = [0]

        def settle(ins):
            steps[0] += 1
            ins.then_inc(pool_step, 1)
            pool.wait_ge(pool_step, steps[0])

        settle(nc.gpsimd.memset(ident[:, :], 0.0))
        nc.gpsimd.affine_select(out=ident[:, :], in_=ident[:, :], compare_op=ALU.not_equal, fill=1.0, base=0,
                                pattern=[[-1, P]], channel_multiplier=1).then_inc(ident_made, 1)
        settle(nc.gpsimd.memset(gate_w[:, :, :], 0.0))
        for g, w in enumerate((w_rgate, w_igate)):
            for t in range(LT):
                for b in range(2):
                    pool.dma_start(gate_w[b * DH:(b + 1) * DH, g * LT + t, b * DH:(b + 1) * DH],
                                   w[0, 2 * t + b, :, :]).then_inc(gate_in, 16)
        nc.gpsimd.memset(xb[:, :, 0:CW - 1], 0.0).then_inc(pad_made, 1)
        settle(nc.gpsimd.memset(eps[:, 0:1], RMS_EPS))
        settle(nc.gpsimd.memset(eps[:, 1:2], LN_EPS))
        settle(nc.gpsimd.memset(blockmean[:, :], 0.0))
        for b in range(2):
            settle(nc.gpsimd.memset(blockmean[b * DH:(b + 1) * DH, b * DH:(b + 1) * DH], 1.0 / DH))
        settle(nc.gpsimd.memset(mask[:, :], 0.0))
        settle(nc.gpsimd.affine_select(out=mask[:, S - P:S], in_=mask[:, S - P:S], compare_op=ALU.is_ge, fill=BIG,
                                       base=0, pattern=[[-1, P]], channel_multiplier=1))
        settle(nc.gpsimd.memset(onehot[:, :], 0.0))
        for b in range(4):
            settle(nc.gpsimd.affine_select(out=onehot[:, :], in_=onehot[:, :], compare_op=ALU.not_equal, fill=1.0,
                                           base=-32 * b, pattern=[[-1, NFOX]], channel_multiplier=1))
        settle(nc.gpsimd.memset(f32(fox_g[:, :]), 0.0))
        settle(nc.gpsimd.memset(f32(fox_k[:, :]), 0.0))
        for b, (buf, v) in enumerate(((fox_g, 1.0), (fox_g, 1.0), (fox_k, -1.0), (fox_k, -1.0))):
            ins = nc.gpsimd.memset(f32(buf[32 * b:32 * b + NFOX, :]), v)
            if b < 3:
                settle(ins)
        ins.then_inc(consts_made, 1)
        pool.wait_ge(fox_ready, 4)
        for p in range(MOBAP, PAIRS):
            pool.wait_ge(scores, score_no(p - 1, ST - 1, 1))
            for h in range(2):
                head = 2 * (p - MOBAP) + h
                nc.gpsimd.tensor_scalar(fox_q[:, h, :], f32(fox_g[:, :]), onehot[:, head:head + 1], None, ALU.mult)\
                  .then_inc(fox_q_done, 1)

    @block.scalar
    def _(act):
        for src, r, n in ((conv_w[0].rearrange("j (t p) -> (j t) p", p=P), R_CONV, CW * LT),
                          (conv_b[0].rearrange("(t p) -> t p", p=P), R_CONVB, LT),
                          (b_rgate[0].rearrange("(t p) -> t p", p=P), R_BR, LT),
                          (b_igate[0].rearrange("(t p) -> t p", p=P), R_BI, LT),
                          (lru_lambda[0].rearrange("(t p) -> t p", p=P), R_LAM, LT),
                          (out_norm_g[0].rearrange("(t p) -> t p", p=P), R_G, YT)):
            act.dma_start(par_rows[r:r + n, :], src).then_inc(par_in, 16)
        act.dma_start(bf[:, :], b_fgate[0].rearrange("(h a) -> h a", a=1)).then_inc(par_in, 16)

        def split_w(u, turn=0):
            act.wait_ge(raw_in[unit(u)], turn * 16 + 16 * (u // SLOTS + 1))
            if u >= SLOTS:
                act.wait_ge(unit_used, turn * 4 + (u - SLOTS + 1))
            nc.scalar.activation(w_hi[:, unit(u), :], raw[:, unit(u), :], ACT.Copy).then_inc(w_hi_done, 1)

        for c in range(DC):
            if c == 4:
                split_w(0)
            act.wait_ge(x_tr, c + 1)
            nc.scalar.activation(a_hi[:, c, :], psum[:, 2 + c % 6, :], ACT.Copy).then_inc(x_hi_done, 1)
        split_w(1)
        for i, v in enumerate((ln1_g, ln1_b)):
            act.dma_start(gb[:, i, :], v[0].partition_broadcast(P)).then_inc(gb_in, 16)
        for t in range(LT):
            split_w(t + 2)
            act.wait_ge(unit_used, t + 1)
            nc.scalar.activation(xb[:, t, CW - 1:], psum[:, t % 2, :], ACT.Copy).then_inc(xb_done, 1)
        for t in range(LT):
            split_w(LT + t + 2)
            act.wait_ge(unit_used, LT + t + 1)
            nc.scalar.activation(lg[:, t, :], psum[:, (LT + t) % 2, :], ACT.Gelu_apprx_tanh).then_inc(gelu_done, 1)
        act.wait_ge(gates_mm, 1)
        act.wait_ge(par_done, 1)
        for g in range(2):
            for t in range(LT):
                b = (R_BR, R_BI)[g] + t
                nc.scalar.activation(ri[:, g, t, :], psum[:, 2 + g * LT + t, :], ACT.Sigmoid,
                                     bias=par[:, b:b + 1]).then_inc(gates_done, 1)
        split_w(U_FF + 2)
        nc.scalar.activation(lam[:, 0, :], par[:, R_LAM:R_LAM + LT], ACT.Abs).then_inc(logexp_done, 1)
        act.wait_ge(logexp_done, 1)
        nc.scalar.activation(lam[:, 1, :], lam[:, 0, :], ACT.Exp, scale=-1.0).then_inc(logexp_done, 1)
        act.wait_ge(unit_used, U_FF + 1)
        act.wait_ge(par_in, 16 * PAR_DMAS)
        nc.scalar.activation(fg[:, 0, :], psum[0:NFOX, U_FF % 2, :], ACT.Abs, bias=bf[:, 0:1]).then_inc(logexp_done, 1)
        act.wait_ge(logexp_done, 3)
        nc.scalar.activation(fg[:, 1, :], fg[:, 0, :], ACT.Exp, scale=-1.0).then_inc(logexp_done, 1)
        split_w(U_QKV + 2)
        act.wait_ge(log_decay_done, 2)
        act.wait_ge(gates_done, LT)
        for t in range(LT):
            nc.scalar.activation(a_t[:, t, :], ri[:, 0, t, :], ACT.Exp, scale=lam[:, 6, t:t + 1]).then_inc(decay_done, 1)
            nc.scalar.activation(th[:, t, :], ri[:, 0, t, :], ACT.Tanh, scale=lam[:, 7, t:t + 1]).then_inc(decay_done, 1)

        act.wait_ge(root_arg, 1)
        nc.scalar.activation(th[:, :, :], th[:, :, :], ACT.Sqrt).then_inc(root_done, 1)

        def q_high(p, u):
            act.wait_ge(unit_used, u + 1)
            nc.scalar.activation(q_hi[:, p % 2, :], psum[:, u % 2, :], ACT.Copy, scale=-SCALE).then_inc(q_hi_done, 1)

        def k_high(p, u):
            act.wait_ge(unit_used, u + 1)
            nc.scalar.activation(k_hi[:, p % 2, :], psum[:, u % 2, :], ACT.Copy).then_inc(k_hi_done, 1)

        def v_copy(p, u):
            act.wait_ge(unit_used, u + 1)
            if p >= 1:
                act.wait_ge(v_tr, p)
            nc.scalar.activation(vT[:, :], psum[:, u % 2, :], ACT.Copy).then_inc(vT_done, 1)

        def square(n):
            wait_y(act, n)
            if n >= 1:
                act.wait_ge(ms_mm, n)
            nc.scalar.activation(sq[:, :], yraw[:, n % 2, :], ACT.Square).then_inc(sq_done, 1)

        def rms(n):
            act.wait_ge(ms_mm, n + 1)
            if n >= 1:
                act.wait_ge(yn_done, n)
            nc.scalar.activation(rstd[:, :], psum[:, B_OUT, :], ACT.Ln, bias=eps[:, 0:1]).then_inc(ms_read, 1)
            act.wait_ge(ms_read, n + 1)
            nc.scalar.activation(rstd[:, :], rstd[:, :], ACT.Exp, scale=-0.5).then_inc(rstd_done, 1)

        def rstd_rows(n, s):
            k = n * ST + s
            act.wait_ge(var_done, k + 1)
            r = rstd_ln[:, s % 2:s % 2 + 1]
            nc.scalar.activation(r, mv[:, s % 2, 1:2], ACT.Ln, bias=eps[:, 1:2]).then_inc(var_log, 1)
            act.wait_ge(var_log, k + 1)
            nc.scalar.activation(r, r, ACT.Exp, scale=-0.5).then_inc(rstd_ln_done, 1)

        def y_high(n):
            act.wait_ge(yn_done, n + 1)
            act.wait_ge(unit_used, U_OUT)
            nc.scalar.activation(a_hi[:, n, :], yn[:, n, :], ACT.Copy).then_inc(y_hi_done, 1)

        def exponentials(p, i):
            for h in range(2):
                n = score_no(p, i, h)
                act.wait_ge(masked, n)
                if n > 2:
                    act.wait_ge(p_tr, n - 2)
                nc.scalar.activation(prob[:, h, 0:(i + 1) * P], smask[:, h, 0:(i + 1) * P], ACT.Exp, scale=-1.0,
                                     bias=nmax[:, h:h + 1], accum_out=rsum[:, h:h + 1]).then_inc(exps, 1)

        def transposed_hi(p, i):
            for h in range(2):
                act.wait_ge(p_tr, score_no(p, i, h))
                if i == 0 and p >= 1:
                    act.wait_ge(pv_done, 2 * (p - 1) + h + 1)
                nc.scalar.activation(by_key(pt_hi, h, i), blocks(B_TRANS + h, i + 1), ACT.Copy).then_inc(pt_hi_done, 1)

        def attend(p, u):
            more = p + 1 < PAIRS
            if not more:
                y_high(0)
            act.wait_ge(v_tr, p + 1)
            if p >= 1:
                act.wait_ge(pv_done, 2 * p)
            nc.scalar.activation(heads(0), v_blocks(), ACT.Copy).then_inc(v_hi_done, 1)
            exponentials(p, 0)
            square(p + 1)
            split_w(u + 2)
            exponentials(p, 1)
            transposed_hi(p, 0)
            if not more:
                y_high(1)
                y_high(2)
            exponentials(p, 2)
            transposed_hi(p, 1)
            rms(p + 1)
            if more:
                q_high(p + 1, u)
            split_w(u + 3)
            exponentials(p, 3)
            transposed_hi(p, 2)
            if more:
                k_high(p + 1, u + 1)
                split_w(u + 4)
            else:
                y_high(3)
            transposed_hi(p, 3)
            if more:
                v_copy(p + 1, u + 2)
            for h in range(2):
                act.wait_ge(pv_done, 2 * p + h + 1)
                if 2 * p + h >= 1:
                    act.wait_ge(half_added, 2 * p + h)
                nc.scalar.activation(otmp[:, :], psum[DH:P, B_OUT + h, :], ACT.Copy).then_inc(o_copied, 1)

        act.wait_ge(consts_made, 1)
        q_high(0, U_QKV)
        split_w(U_QKV + 3)
        square(0)
        k_high(0, U_QKV + 1)
        rms(0)
        split_w(U_QKV + 4)
        v_copy(0, U_QKV + 2)
        for p in range(PAIRS):
            attend(p, U_QKV + 3 * (p + 1))
        for n in range(LT + 2, NORMS - 1):
            y_high(n)
        square(NORMS - 1)
        rms(NORMS - 1)
        y_high(NORMS - 1)
        for n in range(SLOTS, YT):
            split_w(U_OUT + n)

        def x1_high(s):
            act.wait_ge(x1_tr, s + 1)
            nc.scalar.activation(a_hi[:, :, s * P:(s + 1) * P],
                                 psum[:, 2 * s:2 * s + 2, :].rearrange("p b (c n) -> p (b c) n", n=P),
                                 ACT.Copy).then_inc(x1_hi_done, 1)

        rstd_rows(0, 0)
        for s in range(1, ST - 1):
            rstd_rows(0, s)
            x1_high(s - 1)
        split_w(U_FFN)
        split_w(U_FFN + 1)
        rstd_rows(0, ST - 1)
        x1_high(ST - 2)
        x1_high(ST - 1)

        def ffn_turn(it):
            for f in range(2):
                for k in range(2):
                    split_w(U_FFN + 2 + 2 * f + k, it)
                act.wait_ge(unit_used, it * 4 + (U_FFN + 2 * f + 1))
                if it is not first:
                    act.wait_ge(hid_done, it * 2 + (f - 1))
                nc.scalar.activation(silu[:, f, :], psum[:, 2 * f, :], ACT.Silu).then_inc(silu_done, 1)

        first = 0
        ffn_turn(first)
        with act.Fori(1, FT // 2) as it:
            ffn_turn(it)

        def split_h(f, turn=0):
            if f >= SLOTS:
                act.wait_ge(unit_used, turn * 4 + (U_DOWN + f - SLOTS + 1))
            act.wait_ge(hid_done, turn * 4 + (f + 1))
            nc.scalar.activation(h_hi[:, f % SLOTS, :], hid[:, bass.ds(turn * (4 * S) + f * S, S)], ACT.Copy)\
              .then_inc(h_hi_done, 1)

        split_h(0)
        split_h(1)
        for f in range(2, 4):
            split_w(U_DOWN + f)
            split_h(f)
        with act.Fori(0, DOWN_TURNS) as it:
            for f in range(4, 8):
                split_w(U_DOWN + f, it)
                split_h(f, it)
        for f in range(FT - 2, FT):
            split_w(U_DOWN + f)
            split_h(f)
        for s in range(ST):
            rstd_rows(1, s)

    @block.vector
    def _(dve):
        steps = [0]

        def step(ins):
            steps[0] += 1
            ins.then_inc(dve_step, 1)

        def settled():
            dve.wait_ge(dve_step, steps[0])

        def split_w(u, turn=0):
            dve.wait_ge(w_hi_done, turn * 4 + (u + 1))
            nc.vector.tensor_tensor(w_lo[:, unit(u), :], raw[:, unit(u), :], f32(w_hi[:, unit(u), :]), ALU.subtract)\
              .then_inc(w_lo_done, 1)

        def log_sigmoid(t):
            step(nc.vector.tensor_scalar(t(3), t(1), 2.0, None, ALU.add))
            settled()
            step(nc.vector.reciprocal(t(4), t(3)))
            settled()
            step(nc.vector.tensor_tensor(t(3), t(1), t(4), ALU.mult))
            settled()
            step(nc.vector.tensor_tensor(t(4), t(3), t(3), ALU.mult))
            settled()
            step(nc.vector.tensor_scalar(t(5), t(4), ATANH[-1], None, ALU.mult))
            for c in reversed(ATANH[:-1]):
                settled()
                step(nc.vector.scalar_tensor_tensor(t(5), t(5), c, t(4), ALU.add, ALU.mult))
            settled()
            step(nc.vector.scalar_tensor_tensor(t(5), t(5), 1.0, t(3), ALU.add, ALU.mult))
            settled()
            step(nc.vector.scalar_tensor_tensor(t(0), t(5), -2.0, t(2), ALU.mult, ALU.add))
            settled()

        dve.wait_ge(par_tr, 1)
        nc.vector.tensor_copy(par[:, 0:NPAR], psum[:, 1, 0:NPAR]).then_inc(par_done, 1)
        for c in range(DC):
            if c == 4:
                split_w(0)
            dve.wait_ge(x_hi_done, c + 1)
            nc.vector.tensor_tensor(a_lo[:, c, :], psum[:, 2 + c % 6, :], f32(a_hi[:, c, :]), ALU.subtract)\
              .then_inc(x_lo_done, 1)
        split_w(1)
        dve.wait_ge(par_done, 1)
        for t in range(LT):
            split_w(t + 2)
            dve.wait_ge(xb_done, t + 1)
            dve.wait_ge(pad_made, 1)

            def tap(j):
                n = R_CONV + j * LT + t
                return xb[:, t, j:j + S], par[:, n:n + 1]

            src, w = tap(CW - 1)
            step(nc.vector.tensor_scalar(xc[:, t, :], src, w, par[:, R_CONVB + t:R_CONVB + t + 1], ALU.mult, ALU.add))
            for j in reversed(range(CW - 1)):
                src, w = tap(j)
                settled()
                ins = nc.vector.scalar_tensor_tensor(xc[:, t, :], src, w, xc[:, t, :], ALU.mult, ALU.add)
                if j:
                    step(ins)
            ins.then_inc(conv_done, 1)
        split_w(LT + 2)
        split_w(LT + 3)
        split_w(LT + 4)
        dve.wait_ge(logexp_done, 2)
        step(nc.vector.tensor_scalar(lam[:, 2, :], par[:, R_LAM:R_LAM + LT], 0.0, None, ALU.min))
        log_sigmoid(lambda k: lam[:, k, :])
        for k, sign in ((6, 1.0), (7, -1.0)):
            nc.vector.tensor_scalar(lam[:, k, :], lam[:, 0, :], sign * LRU_C, None, ALU.mult).then_inc(log_decay_done, 1)
        dve.wait_ge(logexp_done, 4)
        nc.vector.tensor_scalar(fg[:, 2, :], psum[0:NFOX, U_FF % 2, :], bf[:, 0:1], 0.0, ALU.add, ALU.min)\
          .then_inc(ff_read, 1)
        split_w(U_QKV + 2)
        dve.wait_ge(decay_done, 2 * LT)
        dve.wait_ge(gates_done, 2 * LT)
        sq_a = xb[:, :, 0:S]
        step(nc.vector.tensor_tensor(sq_a, a_t[:, :, :], a_t[:, :, :], ALU.mult))
        settled()
        step(nc.vector.scalar_tensor_tensor(th[:, :, :], sq_a, 1.0, th[:, :, :], ALU.add, ALU.mult))
        settled()
        nc.vector.tensor_scalar(th[:, :, :], th[:, :, :], 1e-32, None, ALU.max).then_inc(root_arg, 1)
        step(nc.vector.tensor_tensor(xc[:, :, :], ri[:, 1, :, :], xc[:, :, :], ALU.mult))
        settled()
        dve.wait_ge(root_done, 1)
        step(nc.vector.tensor_tensor(th[:, :, :], th[:, :, :], xc[:, :, :], ALU.mult))
        settled()
        for t in range(LT):
            step(nc.vector.tensor_tensor_scan(xb[:, t, 0:S], a_t[:, t, :], th[:, t, :], 0.0, ALU.mult, ALU.add))
        dve.wait_ge(gelu_done, LT)
        settled()
        for t in range(LT):
            nc.vector.tensor_tensor(yraw[:, t, :], xb[:, t, 0:S], lg[:, t, :], ALU.mult).then_inc(lru_done, 1)

        def forget_bias():
            dve.wait_ge(ff_read, 1)
            log_sigmoid(lambda k: fg[:, k, :])
            dve.wait_ge(consts_made, 1)
            step(nc.vector.tensor_tensor_scan(fg[:, 1, :], f32(fox_g[0:NFOX, :]), fg[:, 0, :], 0.0, ALU.mult, ALU.add))
            settled()
            nc.vector.tensor_copy(fox_k[0:NFOX, :], fg[:, 1, :]).then_inc(fox_ready, 1)
            nc.vector.tensor_copy(fox_g[64:64 + NFOX, :], fg[:, 1, :]).then_inc(fox_ready, 1)
            dve.wait_ge(fox_ready, 2)
            f_hi = f32(fox_k[0:NFOX, :])
            nc.vector.tensor_tensor(fox_k[32:32 + NFOX, :], fg[:, 1, :], f_hi, ALU.subtract).then_inc(fox_ready, 1)
            nc.vector.tensor_tensor(fox_g[96:96 + NFOX, :], fg[:, 1, :], f_hi, ALU.subtract).then_inc(fox_ready, 1)

        def q_low(p, u):
            dve.wait_ge(q_hi_done, p + 1)
            nc.vector.scalar_tensor_tensor(q_lo[:, p % 2, :], psum[:, u % 2, :], -SCALE, f32(q_hi[:, p % 2, :]),
                                           ALU.mult, ALU.subtract).then_inc(q_lo_done, 1)

        def k_low(p, u):
            dve.wait_ge(k_hi_done, p + 1)
            nc.vector.tensor_tensor(k_lo[:, p % 2, :], psum[:, u % 2, :], f32(k_hi[:, p % 2, :]), ALU.subtract)\
              .then_inc(k_lo_done, 1)

        def norm(n):
            dve.wait_ge(rstd_done, n + 1)
            g = R_G + y_tile[n]
            nc.vector.scalar_tensor_tensor(yn[:, n, :], yraw[:, n % 2, :], par[:, g:g + 1], rstd[:, :],
                                           ALU.mult, ALU.mult).then_inc(yn_done, 1)

        def y_low(n):
            dve.wait_ge(y_hi_done, n + 1)
            nc.vector.tensor_tensor(a_lo[:, n, :], yn[:, n, :], f32(a_hi[:, n, :]), ALU.subtract).then_inc(y_lo_done, 1)

        def mask_scores(p, i):
            w = (i + 1) * P
            for h in range(2):
                n = score_no(p, i, h)
                dve.wait_ge(scores, n)
                if n > 2:
                    dve.wait_ge(exps, n - 2)
                nc.vector.tensor_tensor_reduce(out=smask[:, h, 0:w], in0=psum[:, B_SCORE + h, 0:w], in1=mask[:, S - w:S],
                                               scale=1.0, scalar=BIG, op0=ALU.add, op1=ALU.min,
                                               accum_out=nmax[:, h:h + 1]).then_inc(masked, 1)

        def normalise(p, i):
            for h in range(2):
                dve.wait_ge(exps, score_no(p, i, h))
                step(nc.vector.reciprocal(rinv[:, h:h + 1], rsum[:, h:h + 1]))
            for h in range(2):
                settled()
                row = prob[:, h, 0:(i + 1) * P]
                nc.vector.tensor_scalar(row, row, rinv[:, h:h + 1], None, ALU.mult).then_inc(probs, 1)

        def transposed_lo(p, i):
            for h in range(2):
                dve.wait_ge(pt_hi_done, score_no(p, i, h))
                nc.vector.tensor_tensor(by_key(pt_lo, h, i), blocks(B_TRANS + h, i + 1), f32(by_key(pt_hi, h, i)),
                                        ALU.subtract).then_inc(pt_lo_done, 1)

        def attend(p, u):
            more = p + 1 < PAIRS
            if not more:
                y_low(0)
            dve.wait_ge(v_hi_done, p + 1)
            nc.vector.tensor_tensor(heads(1), v_blocks(), f32(heads(0)), ALU.subtract).then_inc(v_lo_done, 1)
            mask_scores(p, 0)
            split_w(u + 2)
            normalise(p, 0)
            mask_scores(p, 1)
            transposed_lo(p, 0)
            normalise(p, 1)
            mask_scores(p, 2)
            if not more:
                y_low(1)
                y_low(2)
            transposed_lo(p, 1)
            if more:
                q_low(p + 1, u)
            split_w(u + 3)
            normalise(p, 2)
            norm(p + 1)
            mask_scores(p, 3)
            transposed_lo(p, 2)
            normalise(p, 3)
            if more:
                k_low(p + 1, u + 1)
                split_w(u + 4)
            else:
                y_low(3)
            transposed_lo(p, 3)
            for h in range(2):
                dve.wait_ge(o_copied, 2 * p + h + 1)
                nc.vector.tensor_tensor(yraw[h * DH:(h + 1) * DH, (p + LT) % 2, :], psum[0:DH, B_OUT + h, :],
                                        otmp[:, :], ALU.add).then_inc(half_added, 1)

        forget_bias()
        q_low(0, U_QKV)
        split_w(U_QKV + 3)
        norm(0)
        k_low(0, U_QKV + 1)
        split_w(U_QKV + 4)
        for p in range(PAIRS):
            attend(p, U_QKV + 3 * (p + 1))
        for n in range(LT + 2, NORMS - 1):
            y_low(n)
        norm(NORMS - 1)
        y_low(NORMS - 1)
        for n in range(SLOTS, YT):
            split_w(U_OUT + n)

        def layer_norm(n, s, dst, done):
            zs, m = z[:, s % 2, :], mv[:, s % 2, :]
            step(nc.vector.scalar_tensor_tensor(zs.rearrange("p (b n) -> p b n", b=2), x_nat[:, s, :].rearrange("p (b n) -> p b n", b=2),
                                                ALPHA, psum[:, 2 * s:2 * s + 2, :], ALU.mult, ALU.add))
            settled()
            for b in range(D // BN):
                step(nc.vector.bn_stats(stats[:, s % 2, b, :], zs[:, b * BN:(b + 1) * BN]))
            settled()
            nc.vector.bn_aggr(m, stats[:, s % 2, :, :].rearrange("p b k -> p (b k)")).then_inc(var_done, 1)
            dve.wait_ge(rstd_ln_done, n * ST + s + 1)
            r = rstd_ln[:, s % 2:s % 2 + 1]
            step(nc.vector.tensor_scalar(zs, zs, m[:, 0:1], r, ALU.subtract, ALU.mult))
            settled()
            step(nc.vector.tensor_tensor(zs, zs, gb[:, 0, :], ALU.mult))
            settled()
            nc.vector.tensor_tensor(dst, zs, gb[:, 1, :], ALU.add).then_inc(done, 1)

        def x1_low(s):
            dve.wait_ge(x1_hi_done, s + 1)
            cols = a_hi[:, :, s * P:(s + 1) * P]
            nc.vector.tensor_tensor(a_lo[:, :, s * P:(s + 1) * P],
                                    psum[:, 2 * s:2 * s + 2, :].rearrange("p b (c n) -> p (b c) n", n=P),
                                    f32(cols), ALU.subtract).then_inc(x1_lo_done, 1)

        dve.wait_ge(gb_in, 32)
        for s in range(ST):
            if s < ST - 1:
                dve.wait_ge(rows_mixed, s + 1)
            else:
                dve.wait_ge(unit_used, U_FFN)
            layer_norm(0, s, x_nat[:, s, :], x1_done)
            if s >= 1:
                x1_low(s - 1)
            if s == ST - 2:
                split_w(U_FFN)
                split_w(U_FFN + 1)
        x1_low(ST - 1)

        def ffn_turn(it):
            for f in range(2):
                for k in range(2):
                    split_w(U_FFN + 2 + 2 * f + k, it)
                dve.wait_ge(silu_done, it * 2 + (f + 1))
                dve.wait_ge(unit_used, it * 4 + (U_FFN + 2 * f + 2))
                nc.vector.tensor_tensor(hid[:, bass.ds(it * (2 * S) + f * S, S)], psum[:, 2 * f + 1, :], silu[:, f, :],
                                        ALU.mult).then_inc(hid_done, 1)

        ffn_turn(0)
        with dve.Fori(1, FT // 2) as it:
            ffn_turn(it)

        def split_h(f, turn=0):
            dve.wait_ge(h_hi_done, turn * 4 + (f + 1))
            nc.vector.tensor_tensor(h_lo[:, f % SLOTS, :], hid[:, bass.ds(turn * (4 * S) + f * S, S)],
                                    f32(h_hi[:, f % SLOTS, :]), ALU.subtract).then_inc(h_lo_done, 1)

        split_h(0)
        split_h(1)
        for f in range(2, 4):
            split_w(U_DOWN + f)
            split_h(f)
        with dve.Fori(0, DOWN_TURNS) as it:
            for f in range(4, 8):
                split_w(U_DOWN + f, it)
                split_h(f, it)
        for f in range(FT - 2, FT):
            split_w(U_DOWN + f)
            split_h(f)
        dve.wait_ge(gb_in, 64)
        for s in range(ST):
            dve.wait_ge(rows_down, s + 1)
            if s >= 2:
                dve.wait_ge(out_stored[s % 2], 16 * (s // 2))
            layer_norm(1, s, z[:, s % 2, :], out_ready)

    @block.tensor
    def _(pe):
        def three(dst, s_hi, s_lo, m_hi, m_lo, start, stop):
            nc.tensor.matmul(dst, s_hi, m_hi, start=start, stop=False)
            nc.tensor.matmul(dst, s_hi, m_lo, start=False, stop=False)
            return nc.tensor.matmul(dst, s_lo, m_hi, start=False, stop=stop)

        def unit_ready(u, turn=0):
            pe.wait_ge(w_lo_done, turn * 4 + (u + 1))

        def chunk(dst, u, c):
            cols = slice(c * P, (c + 1) * P)
            return three(dst, w_hi[:, unit(u), cols], w_lo[:, unit(u), cols], a_hi[:, c, :], a_lo[:, c, :],
                         c == 0, c == DC - 1)

        def bank_free(u):
            v = u - 2
            if v < 0:
                if u == 1:
                    pe.wait_ge(par_done, 1)
            elif v < LT:
                pe.wait_ge(xb_done, v + 1)
            elif v < 2 * LT:
                pe.wait_ge(gelu_done, v - LT + 1)
            elif v == U_FF:
                pe.wait_ge(ff_read, 1)
            else:
                p, k = divmod(v - U_QKV, 3)
                pe.wait_ge((q_lo_done, k_lo_done, vT_done)[k], p + 1)

        def project(u, quarter):
            if quarter == 0:
                unit_ready(u)
                bank_free(u)
            for c in range(2 * quarter, 2 * quarter + 2):
                if u == 0:
                    pe.wait_ge(x_lo_done, c + 1)
                last = chunk(psum[:, u % 2, :], u, c)
            if quarter == 3:
                last.then_inc(unit_used, 1)

        def gates():
            pe.wait_ge(conv_done, LT)
            pe.wait_ge(gate_in, 16 * 4 * LT)
            for g in range(2):
                for t in range(LT):
                    last = nc.tensor.matmul(psum[:, 2 + g * LT + t, :], gate_w[:, g * LT + t, :], xc[:, t, :],
                                            start=True, stop=True)
            last.then_inc(gates_mm, 1)

        def mean_square(n):
            pe.wait_ge(sq_done, n + 1)
            if n >= 1:
                pe.wait_ge(ms_read, n)
            nc.tensor.matmul(psum[:, B_OUT, :], blockmean[:, :], sq[:, :], start=True, stop=True).then_inc(ms_mm, 1)

        def transpose_v(p):
            pe.wait_ge(vT_done, p + 1)
            if p >= 1:
                pe.wait_ge(pt_lo_done, score_no(p - 1, ST - 1, 0))
            for t in range(ST):
                last = nc.tensor.transpose(psum[:, B_TRANS, t * P:(t + 1) * P], vT[:, t * P:(t + 1) * P], ident[:, :])
            last.then_inc(v_tr, 1)

        def score(p, i):
            w = (i + 1) * P
            if i == 0:
                pe.wait_ge(q_lo_done, p + 1)
                pe.wait_ge(k_lo_done, p + 1)
            for h in range(2):
                n = score_no(p, i, h)
                if n > 2:
                    pe.wait_ge(masked, n - 2)
                dst = psum[:, B_SCORE + h, 0:w]
                rows = slice(h * DH, (h + 1) * DH)
                cols = slice(i * P, (i + 1) * P)
                fox = p >= MOBAP
                if fox:
                    pe.wait_ge(fox_q_done, 2 * (p - MOBAP) + h + 1)
                    nc.tensor.matmul(dst, fox_q[:, h, cols], fox_k[:, 0:w], start=True, stop=False)
                b = p % 2
                three(dst, q_hi[rows, b, cols], q_lo[rows, b, cols], k_hi[rows, b, 0:w], k_lo[rows, b, 0:w],
                      not fox, True).then_inc(scores, 1)

        def transpose_p(p, i):
            for h in range(2):
                n = score_no(p, i, h)
                pe.wait_ge(probs, n)
                if n > 2:
                    pe.wait_ge(pt_lo_done, n - 2)
                if i == 0 and h == 0:
                    pe.wait_ge(v_lo_done, p + 1)
                for j in range(i + 1):
                    last = nc.tensor.transpose(psum[:, B_TRANS + h, j * P:(j + 1) * P], prob[:, h, j * P:(j + 1) * P],
                                               ident[:, :])
                last.then_inc(p_tr, 1)

        def values(p, h):
            pe.wait_ge(pt_lo_done, score_no(p, ST - 1, h))
            pe.wait_ge(ms_read, p + 2)
            if p >= 1:
                pe.wait_ge(half_added, 2 * (p - 1) + h + 1)
            for j in range(ST):
                cols = slice(j * PT_STRIDE + j * P, j * PT_STRIDE + S)
                for buf in (pt_hi, pt_lo):
                    last = nc.tensor.matmul(psum[:, B_OUT + h, j * P:S], vv[:, j, h, :], buf[:, h, cols],
                                            start=(j == 0 and buf is pt_hi), stop=(j == ST - 1 and buf is pt_lo))
            last.then_inc(pv_done, 1)

        def rows_times(s, a_parts, w_slot, first, last_one, only=None):
            hi, lo = (a[:, s * P:(s + 1) * P] for a in a_parts)
            steps = [(hi, w_hi, 0), (hi, w_hi, 1), (hi, w_lo, 0), (hi, w_lo, 1), (lo, w_hi, 0), (lo, w_hi, 1)]
            for k in (only if only is not None else range(6)):
                a, w, half = steps[k]
                last = nc.tensor.matmul(psum[:, 2 * s + half, :], a, w[:, w_slot, half * S:(half + 1) * S],
                                        start=first and k < 2, stop=last_one and k >= 4)
            return last

        def mix_rows(s, n, only=None):
            if s == 0 or n >= SLOTS:
                unit_ready(U_OUT + n)
                pe.wait_ge(y_lo_done, n + 1)
            return rows_times(s, (a_hi[:, n, :], a_lo[:, n, :]), unit(U_OUT + n), n == 0, n == YT - 1, only)

        def attend(p, beside):
            take = iter(beside)

            def piece(n=1):
                for _ in range(n):
                    next(take)()

            piece()
            transpose_v(p)
            score(p, 0)
            piece()
            score(p, 1)
            piece()
            transpose_p(p, 0)
            score(p, 2)
            mean_square(p + 1)
            piece()
            transpose_p(p, 1)
            piece()
            score(p, 3)
            piece()
            transpose_p(p, 2)
            piece(2)
            transpose_p(p, 3)
            piece(2)
            values(p, 0)
            piece()
            values(p, 1)
            piece()

        pe.wait_ge(ident_made, 1)
        pe.wait_ge(par_in, 16 * PAR_DMAS)
        nc.tensor.transpose(psum[:, 1, 0:NPAR], par_rows[0:NPAR, :], ident[0:NPAR, 0:NPAR]).then_inc(par_tr, 1)
        for c in range(DC):
            pe.wait_ge(x_in[c * ST // DC], 16)
            if c >= 6:
                pe.wait_ge(x_lo_done, c - 5)
            for t in range(ST):
                last = nc.tensor.transpose(psum[:, 2 + c % 6, t * P:(t + 1) * P], x_nat[:, t, c * P:(c + 1) * P],
                                           ident[:, :])
            last.then_inc(x_tr, 1)
        for u in range(U_FF):
            for quarter in range(4):
                project(u, quarter)
            if u == U_FF - 2:
                gates()
        for u in range(U_FF, U_QKV + 3):
            for quarter in range(4):
                project(u, quarter)
            if u == U_QKV + 1:
                mean_square(0)
        pe.wait_ge(gates_done, 2 * LT)
        for p in range(PAIRS):
            u = U_QKV + 3 * (p + 1)
            if p + 1 < PAIRS:
                beside = [(lambda v=u + k // 4, q=k % 4: project(v, q)) for k in range(12)]
            else:
                beside = [(lambda n=k // 3, t=k % 3: mix_rows(0, n, (2 * t, 2 * t + 1))) for k in range(12)]
            attend(p, beside)
        pe.wait_ge(masked, score_no(PAIRS - 1, ST - 1, 1))
        for n in range(SLOTS):
            mix_rows(1, n)
        mean_square(NORMS - 1)
        pe.wait_ge(pt_lo_done, score_no(PAIRS - 1, ST - 1, 1))
        for n in range(SLOTS):
            mix_rows(2, n)
        pe.wait_ge(ms_read, NORMS)
        for n in range(SLOTS):
            mix_rows(3, n).then_inc(unit_used, 1)

        def transpose_x1(s):
            pe.wait_ge(x1_done, s + 1)
            for c in range(DC):
                last = nc.tensor.transpose(psum[:, 2 * s + c // 4, (c % 4) * P:(c % 4 + 1) * P],
                                           x_nat[:, s, c * P:(c + 1) * P], ident[:, :])
            last.then_inc(x1_tr, 1)

        for s in range(ST):
            for n in range(SLOTS, YT):
                last = mix_rows(s, n)
                if s == ST - 1:
                    last.then_inc(unit_used, 1)
            if s < ST - 1:
                last.then_inc(rows_mixed, 1)
            if s >= 1:
                transpose_x1(s - 1)
        transpose_x1(ST - 1)

        pe.wait_ge(x1_lo_done, ST)

        def ffn_turn(it):
            for k in range(4):
                unit_ready(U_FFN + k, it)
                if it is not first:
                    pe.wait_ge((silu_done, hid_done)[k % 2], it * 2 + (k // 2 - 1))
                for c in range(DC):
                    last = chunk(psum[:, k, :], U_FFN + k, c)
                last.then_inc(unit_used, 1)

        first = 0
        ffn_turn(first)
        with pe.Fori(1, FT // 2) as it:
            ffn_turn(it)

        pe.wait_ge(silu_done, FT)
        pe.wait_ge(hid_done, FT)

        def down(f, s, turn=0):
            return rows_times(s, (h_hi[:, f % SLOTS, :], h_lo[:, f % SLOTS, :]), unit(U_DOWN + f),
                              f == 0, f == FT - 1)

        def down_ready(f, turn=0):
            unit_ready(U_DOWN + f, turn)
            pe.wait_ge(h_lo_done, turn * 4 + (f + 1))

        for f in range(2):
            down_ready(f)
            for s in range(ST):
                last = down(f, s)
            last.then_inc(unit_used, 1)
        with pe.Fori(0, DOWN_TURNS) as it:
            for f in range(2, 6):
                down_ready(f, it)
                for s in range(ST):
                    last = down(f, s)
                last.then_inc(unit_used, 1)
        for s in range(ST):
            for f in range(FT - 4, FT):
                if s == 0:
                    down_ready(f)
                last = down(f, s)
            last.then_inc(rows_down, 1)

    ctx.close()


_INS = ['x', 'w_in', 'b_fgate', 'conv_w', 'conv_b', 'w_rgate', 'b_rgate', 'w_igate', 'b_igate', 'lru_lambda',
        'out_norm_g', 'w_out', 'ln1_g', 'ln1_b', 'w_ffn_gate', 'w_ffn_up', 'w_ffn_down', 'ln2_g', 'ln2_b']


def kernel(**inputs):
    import numpy as np
    import concourse.bacc as bacc
    from concourse.bass_utils import run_bass_kernel_spmd

    nc = bacc.Bacc("TRN2", target_bir_lowering=False, num_devices=1)
    arrays, args = {}, []
    for name in _INS:
        a = np.ascontiguousarray(inputs[name])
        arrays[f"in_{name}_dram"] = a
        args.append(nc.dram_tensor(f"in_{name}_dram", a.shape, mybir.dt.from_np(a.dtype), kind="ExternalInput").ap())
    shape = np.shape(inputs['x'])
    args.append(nc.dram_tensor("out_0_dram", shape, mybir.dt.float32, kind="ExternalOutput").ap())
    hymba_layer(nc, *args)
    r = run_bass_kernel_spmd(nc, [arrays], core_ids=[0])
    return r.results[0]["out_0_dram"]
```

```python
import math
from contextlib import ExitStack

import concourse.bass as bass
from concourse import mybir



def hymba_layer(nc, x, w_in, b_fgate, conv_w, conv_b, w_rgate, b_rgate, w_igate, b_igate, lru_lambda,
                out_norm_g, w_out, ln1_g, ln1_b, w_ffn_gate, w_ffn_up, w_ffn_down, ln2_g, ln2_b, out):
    F32 = mybir.dt.float32
    F32R = mybir.dt.float32r
    ALU = mybir.AluOpType
    ACT = mybir.ActivationFunctionType

    P = 128
    _, S, D = x.shape
    DC = D // P
    ST = S // P
    NFOX = b_fgate.shape[1]
    DH = w_rgate.shape[2]
    DLRU = conv_b.shape[1]
    DFOX = NFOX * DH
    DMOBA = D - DLRU - DFOX
    F = w_ffn_gate.shape[2]
    FT = F // P
    CW = conv_w.shape[1]
    H2 = S
    PAIRS = (DFOX + DMOBA) // P
    FOXP = DFOX // P
    MOBAP = DMOBA // P
    LT = DLRU // P
    YT = D // P
    ALPHA = 2 ** 0.25
    SCALE = 1.0 / math.sqrt(DH)
    BIG = 1e30
    LRU_C = 8.0
    LN_EPS = 1e-5
    RMS_EPS = 1e-6
    BN = 512

    C_FQ, C_FK, C_FV, C_FF = 0, DFOX, 2 * DFOX, 3 * DFOX
    C_MQ = C_FF + NFOX
    C_MK = C_MQ + DMOBA
    C_MV = C_MK + DMOBA
    C_LX = C_MV + DMOBA
    C_LG = C_LX + DLRU

    U_FF = 2 * LT
    U_QKV = U_FF + 1
    U_OUT = U_QKV + 3 * PAIRS
    U_FFN = U_OUT + YT
    U_DOWN = U_FFN + 2 * FT
    SLOTS = 4
    proj_col = [C_LX + P * t for t in range(LT)] + [C_LG + P * t for t in range(LT)] + [C_FF]
    for p in range(MOBAP):
        proj_col += [C_MQ + P * p, C_MK + P * p, C_MV + P * p]
    for p in range(FOXP):
        proj_col += [C_FQ + P * p, C_FK + P * p, C_FV + P * p]
    y_tile = [FOXP + MOBAP + t for t in range(LT)]
    y_tile += [FOXP + p for p in range(MOBAP)] + [p for p in range(FOXP)]
    NORMS = YT
    out_tiles = list(y_tile)

    assert max(-(-S // 256), 3) == 3

    ctx = ExitStack()
    common = ctx.enter_context(ExitStack())

    def sb(stack, name, shape, dt=F32):
        return stack.enter_context(nc.sbuf_tensor(name, shape, dt))

    def sem(name):
        return ctx.enter_context(nc.semaphore(name))

    raw = sb(common, "raw", [P, SLOTS, D])
    w_hi = sb(common, "w_hi", [P, SLOTS, D], F32R)
    w_lo = sb(common, "w_lo", [P, SLOTS, D], F32R)
    a_hi = sb(common, "a_hi", [P, DC, S], F32R)
    a_lo = sb(common, "a_lo", [P, DC, S], F32R)
    x_nat = sb(common, "x_nat", [P, ST, D])
    gb = sb(common, "gb", [P, 2, D])
    ident = sb(common, "ident", [P, P])
    stats = sb(common, "stats", [P, 2, D // BN, 6])
    mv = sb(common, "mv", [P, 2, 2])
    eps = sb(common, "eps", [P, 2])
    rstd_ln = sb(common, "rstd_ln", [P, 2])
    root_t = sb(common, "root_t", [P, 2, 4])

    mix = ExitStack()
    q_hi = sb(mix, "q_hi", [P, 2, S], F32R)
    q_lo = sb(mix, "q_lo", [P, 2, S], F32R)
    k_hi = sb(mix, "k_hi", [P, 2, S], F32R)
    k_lo = sb(mix, "k_lo", [P, 2, S], F32R)
    vT = sb(mix, "vT", [P, S])
    vv = sb(mix, "vv", [P, ST, 2, 2 * DH], F32R)
    yraw = sb(mix, "yraw", [P, 2, S])
    otmp = sb(mix, "otmp", [DH, S])
    sq = sb(mix, "sq", [P, S])
    rstd = sb(mix, "rstd", [P, S])
    yn = sb(mix, "yn", [P, YT, S])
    mask = sb(mix, "mask", [P, S])
    blockmean = sb(mix, "blockmean", [P, P])
    gate_w = sb(mix, "gate_w", [P, 2 * LT, P])
    par_rows = sb(mix, "par_rows", [P, P])
    par = sb(mix, "par", [P, 32])
    lam = sb(mix, "lam", [P, 8, LT])
    fox_q = sb(mix, "fox_q", [P, 2, S], F32R)
    fox_g = sb(mix, "fox_g", [P, S], F32R)
    fox_k = sb(mix, "fox_k", [P, S], F32R)
    onehot = sb(mix, "onehot", [P, NFOX])
    bf = sb(mix, "bf", [NFOX, 1])
    nmax = sb(mix, "nmax", [P, 2])
    rsum = sb(mix, "rsum", [P, 2])
    rinv = sb(mix, "rinv", [P, 2])

    lru = ExitStack()
    xb = sb(lru, "xb", [P, LT, CW - 1 + S])
    ri = sb(lru, "ri", [P, 2, LT, S])
    xc = sb(lru, "xc", [P, LT, S])
    a_t = sb(lru, "a_t", [P, LT, S])
    th = sb(lru, "th", [P, LT, S])
    lru.close()
    att = ExitStack()
    PT_STRIDE = S - P
    PT_COLS = (ST - 1) * PT_STRIDE + S
    pt_hi = sb(att, "pt_hi", [P, 2, PT_COLS], F32R)
    pt_lo = sb(att, "pt_lo", [P, 2, PT_COLS], F32R)
    smask = sb(att, "smask", [P, 2, S])
    prob = sb(att, "prob", [P, 2, 2, S])
    att.close()
    mix.close()

    ffn = ExitStack()
    hid = sb(ffn, "hid", [P, FT * S])
    h_hi = sb(ffn, "h_hi", [P, SLOTS, S], F32R)
    h_lo = sb(ffn, "h_lo", [P, SLOTS, S], F32R)
    silu = sb(ffn, "silu", [P, 2, S])
    z = sb(ffn, "z", [P, 2, D])
    ffn.close()

    lg = yn[:, YT - 2 - LT:YT - 2, :]

    def fg(k):
        return gb[0:NFOX, k // 2, k % 2 * S:(k % 2 + 1) * S] if k < 4 else yn[0:NFOX, YT + 3 - k, :]


    psum = ctx.enter_context(nc.psum_tensor("psum", [P, 8, H2], F32))
    B_SCORE, B_TRANS, B_OUT = 2, 4, 6

    x_in = [sem(f"x_in{g}") for g in range(ST)]
    raw_in = [sem(f"raw_in{i}") for i in range(SLOTS)]
    par_in = sem("par_in")
    gate_in = sem("gate_in")
    gb_in = sem("gb_in")
    pad_made = sem("pad_made")
    ident_made = sem("ident_made")
    consts_made = sem("consts_made")
    pool_step = sem("pool_step")
    x_tr = sem("x_tr")
    x_hi_done = sem("x_hi_done")
    x_lo_done = sem("x_lo_done")
    w_hi_done = sem("w_hi_done")
    w_lo_done = sem("w_lo_done")
    unit_used = sem("unit_used")
    par_tr = sem("par_tr")
    par_done = sem("par_done")
    xb_done = sem("xb_done")
    conv_done = sem("conv_done")
    gates_mm = sem("gates_mm")
    gates_done = sem("gates_done")
    gelu_done = sem("gelu_done")
    decay_done = sem("decay_done")
    logexp_done = sem("logexp_done")
    log_decay_done = sem("log_decay_done")
    ff_read = sem("ff_read")
    forget_log = sem("forget_log")
    forget_sum = sem("forget_sum")
    fox_ready = sem("fox_ready")
    fox_q_done = sem("fox_q_done")
    lru_done = sem("lru_done")
    sq_done = sem("sq_done")
    ms_mm = sem("ms_mm")
    ms_read = sem("ms_read")
    yn_done = sem("yn_done")
    q_hi_done = sem("q_hi_done")
    k_hi_done = sem("k_hi_done")
    q_lo_done = sem("q_lo_done")
    k_lo_done = sem("k_lo_done")
    vT_done = sem("vT_done")
    v_tr = sem("v_tr")
    v_hi_done = sem("v_hi_done")
    v_lo_done = sem("v_lo_done")
    scores = sem("scores")
    masked = sem("masked")
    exps = sem("exps")
    probs = sem("probs")
    p_tr = sem("p_tr")
    pt_hi_done = sem("pt_hi_done")
    pt_lo_done = sem("pt_lo_done")
    pv_done = sem("pv_done")
    o_copied = sem("o_copied")
    half_added = sem("half_added")
    y_hi_done = sem("y_hi_done")
    y_lo_done = sem("y_lo_done")
    rows_mixed = sem("rows_mixed")
    sum_done = sem("sum_done")
    x1_done = sem("x1_done")
    x1_tr = sem("x1_tr")
    x1_hi_done = sem("x1_hi_done")
    x1_lo_done = sem("x1_lo_done")
    silu_done = sem("silu_done")
    hid_done = sem("hid_done")
    h_hi_done = sem("h_hi_done")
    h_lo_done = sem("h_lo_done")
    root_arg = sem("root_arg")
    root_done = sem("root_done")
    rstd_done = sem("rstd_done")
    var_done = sem("var_done")
    var_log = sem("var_log")
    rstd_ln_done = sem("rstd_ln_done")
    out_ready = sem("out_ready")
    out_stored = [sem("out_stored0"), sem("out_stored1")]
    rows_down = sem("rows_down")
    dve_step = sem("dve_step")

    w_in_v = w_in[0].rearrange("(c p) n -> p c n", p=P)
    gate_v = w_ffn_gate[0].rearrange("(c p) n -> p c n", p=P)
    up_v = w_ffn_up[0].rearrange("(c p) n -> p c n", p=P)
    x_v = x[0].rearrange("(t p) d -> p t d", p=P)
    out_v = out[0].rearrange("(t p) d -> p t d", p=P)

    def f32(ap):
        return ap.bitcast(F32)

    def unit(u):
        return u % SLOTS

    def score_no(p, i, h):
        return (p * ST + i) * 2 + h + 1

    def by_key(buf, h, i):
        row = buf[:, h, i * P:(i + 1) * P]
        return bass.AP(row.tensor, row.offset, [row.ap[0], [PT_STRIDE, i + 1], [1, P]])

    def blocks(bank, n):
        return psum[:, bank, 0:n * P].rearrange("p (j c) -> p j c", c=P)

    def x1_blocks(s, b):
        return psum[:, 2 * s + b, :].rearrange("p (c n) -> p c n", n=P)

    def heads(part):
        return vv[:, :, :, part * DH:(part + 1) * DH]

    def v_blocks():
        return psum[:, B_TRANS, :].rearrange("p (t h c) -> p t h c", t=ST, h=2)

    def wait_y(eng, n):
        if n < LT:
            eng.wait_ge(lru_done, n + 1)
        else:
            eng.wait_ge(half_added, 2 * (n - LT) + 2)

    R_CONV, R_CONVB, R_BR = 0, CW * LT, (CW + 1) * LT
    R_BI, R_LAM, R_G = R_BR + LT, R_BR + 2 * LT, R_BR + 3 * LT
    NPAR = R_G + YT
    PAR_DMAS = 7
    DOWN_TURNS = (FT - 6) // 4

    ATANH = [1.0 / (2 * n + 1) for n in range(1, 9)]

    block = ctx.enter_context(nc.Block())

    @block.sync
    def _(sp):
        def load(u, dst, src):
            if u >= SLOTS:
                sp.wait_ge(w_lo_done, u - SLOTS + 1)
            sp.dma_start(dst, src).then_inc(raw_in[unit(u)], 16)

        def by_chunk(u):
            return raw[:, unit(u), :].rearrange("p (c n) -> p c n", c=DC)

        W = D // ST
        for g in range(ST):
            sp.dma_start(x_nat[:, :, g * W:(g + 1) * W], x_v[:, :, g * W:(g + 1) * W]).then_inc(x_in[g], 16)
            if g == 0:
                load(0, by_chunk(0), w_in_v[:, :, proj_col[0]:proj_col[0] + P])
        for u in range(1, U_OUT):
            load(u, by_chunk(u), w_in_v[:, :, proj_col[u]:proj_col[u] + P])
        sp.wait_ge(fox_ready, 4)
        for i, v in enumerate((ln1_g, ln1_b)):
            sp.dma_start(gb[:, i, :], v[0].partition_broadcast(P)).then_inc(gb_in, 16)
        for n, m in enumerate(out_tiles):
            load(U_OUT + n, raw[:, unit(U_OUT + n), :], w_out[0, m * P:(m + 1) * P, :])
        with sp.Fori(0, FT // 2) as it:
            for k in range(4):
                u = U_FFN + k
                sp.wait_ge(w_lo_done, it * 4 + (u - SLOTS + 1))
                sp.dma_start(by_chunk(u), (gate_v, up_v)[k % 2][:, :, bass.ds(it * (2 * P) + (k // 2) * P, P)])\
                  .then_inc(raw_in[unit(u)], 16)
        for i, v in enumerate((ln2_g, ln2_b)):
            sp.wait_ge(x1_done, 2 * ST)
            sp.dma_start(gb[:, i, :], v[0].partition_broadcast(P)).then_inc(gb_in, 16)
        for f in range(FT):
            load(U_DOWN + f, raw[:, unit(U_DOWN + f), :], w_ffn_down[0, f * P:(f + 1) * P, :])
        for s in range(ST):
            for b in range(2 if s < ST - 1 else 1):
                cols = slice(b * BN, (b + 1) * BN)
                sp.wait_ge(out_ready, 2 * s + b + 1)
                sp.dma_start(out_v[:, s, cols], z[:, s % 2, cols]).then_inc(out_stored[s % 2], 16)
        for b in range(2):
            sp.wait_ge(out_stored[b], 32 * (ST // 2))

    @block.gpsimd
    def _(pool):
        steps = [0]

        def settle(ins):
            steps[0] += 1
            ins.then_inc(pool_step, 1)
            pool.wait_ge(pool_step, steps[0])

        settle(nc.gpsimd.memset(ident[:, :], 0.0))
        nc.gpsimd.affine_select(out=ident[:, :], in_=ident[:, :], compare_op=ALU.not_equal, fill=1.0, base=0,
                                pattern=[[-1, P]], channel_multiplier=1).then_inc(ident_made, 1)
        settle(nc.gpsimd.memset(gate_w[:, :, :], 0.0))
        for g, w in enumerate((w_rgate, w_igate)):
            for t in range(LT):
                for b in range(2):
                    pool.dma_start(gate_w[b * DH:(b + 1) * DH, g * LT + t, b * DH:(b + 1) * DH],
                                   w[0, 2 * t + b, :, :]).then_inc(gate_in, 16)
        nc.gpsimd.memset(xb[:, :, 0:CW - 1], 0.0).then_inc(pad_made, 1)
        settle(nc.gpsimd.memset(eps[:, 0:1], RMS_EPS))
        settle(nc.gpsimd.memset(eps[:, 1:2], LN_EPS))
        settle(nc.gpsimd.memset(blockmean[:, :], 0.0))
        for b in range(2):
            settle(nc.gpsimd.memset(blockmean[b * DH:(b + 1) * DH, b * DH:(b + 1) * DH], 1.0 / DH))
        settle(nc.gpsimd.memset(mask[:, :], 0.0))
        settle(nc.gpsimd.affine_select(out=mask[:, S - P:S], in_=mask[:, S - P:S], compare_op=ALU.is_ge, fill=BIG,
                                       base=0, pattern=[[-1, P]], channel_multiplier=1))
        settle(nc.gpsimd.memset(onehot[:, :], 0.0))
        for b in range(4):
            settle(nc.gpsimd.affine_select(out=onehot[:, :], in_=onehot[:, :], compare_op=ALU.not_equal, fill=1.0,
                                           base=-32 * b, pattern=[[-1, NFOX]], channel_multiplier=1))
        settle(nc.gpsimd.memset(f32(fox_g[:, :]), 0.0))
        settle(nc.gpsimd.memset(f32(fox_k[:, :]), 0.0))
        for b, (buf, v) in enumerate(((fox_g, 1.0), (fox_g, 1.0), (fox_k, -1.0), (fox_k, -1.0))):
            ins = nc.gpsimd.memset(f32(buf[32 * b:32 * b + NFOX, :]), v)
            if b < 3:
                settle(ins)
        ins.then_inc(consts_made, 1)
        def add_times(dst, a, c, b):
            settle(nc.gpsimd.tensor_scalar(fg(0), a, c, None, ALU.add))
            settle(nc.gpsimd.tensor_tensor(dst, fg(0), b, ALU.mult))

        pool.wait_ge(logexp_done, 4)
        pool.wait_ge(ff_read, 1)
        settle(nc.gpsimd.tensor_scalar(fg(3), fg(1), 8.0 / 49, -24.0 / 49, ALU.mult, ALU.add))
        for _ in range(3):
            add_times(fg(4), fg(1), 2.0, fg(3))
            add_times(fg(3), fg(4), 2.0, fg(3))
        settle(nc.gpsimd.tensor_tensor(fg(3), fg(1), fg(3), ALU.mult))
        settle(nc.gpsimd.tensor_tensor(fg(4), fg(3), fg(3), ALU.mult))
        settle(nc.gpsimd.tensor_scalar(fg(5), fg(4), ATANH[-1], None, ALU.mult))
        for c in reversed(ATANH[:-1]):
            add_times(fg(5), fg(5), c, fg(4))
        add_times(fg(5), fg(5), 1.0, fg(3))
        settle(nc.gpsimd.tensor_scalar(fg(5), fg(5), 2.0, None, ALU.mult))
        nc.gpsimd.tensor_tensor(fg(0), fg(5), fg(2), ALU.add).then_inc(forget_log, 1)
        pool.wait_ge(forget_sum, 1)
        f_hi = f32(fox_k[0:NFOX, :])
        nc.gpsimd.tensor_copy(fox_k[0:NFOX, :], fg(1)).then_inc(fox_ready, 1)
        nc.gpsimd.tensor_copy(fox_g[64:64 + NFOX, :], fg(1)).then_inc(fox_ready, 1)
        pool.wait_ge(fox_ready, 2)
        nc.gpsimd.tensor_tensor(fox_k[32:32 + NFOX, :], fg(1), f_hi, ALU.subtract).then_inc(fox_ready, 1)
        nc.gpsimd.tensor_tensor(fox_g[96:96 + NFOX, :], fg(1), f_hi, ALU.subtract).then_inc(fox_ready, 1)
        pool.wait_ge(fox_ready, 4)
        for p in range(MOBAP, PAIRS):
            pool.wait_ge(scores, score_no(p - 1, ST - 1, 1))
            for h in range(2):
                head = 2 * (p - MOBAP) + h
                nc.gpsimd.tensor_scalar(fox_q[:, h, :], f32(fox_g[:, :]), onehot[:, head:head + 1], None, ALU.mult)\
                  .then_inc(fox_q_done, 1)
        for u in range(U_FFN, U_FFN + 2):
            pool.wait_ge(w_hi_done, u + 1)
            nc.gpsimd.tensor_tensor(w_lo[:, unit(u), :], raw[:, unit(u), :], f32(w_hi[:, unit(u), :]), ALU.subtract)\
              .then_inc(w_lo_done, 1)

    @block.scalar
    def _(act):
        for src, r, n in ((conv_w[0].rearrange("j (t p) -> (j t) p", p=P), R_CONV, CW * LT),
                          (conv_b[0].rearrange("(t p) -> t p", p=P), R_CONVB, LT),
                          (b_rgate[0].rearrange("(t p) -> t p", p=P), R_BR, LT),
                          (b_igate[0].rearrange("(t p) -> t p", p=P), R_BI, LT),
                          (lru_lambda[0].rearrange("(t p) -> t p", p=P), R_LAM, LT),
                          (out_norm_g[0].rearrange("(t p) -> t p", p=P), R_G, YT)):
            act.dma_start(par_rows[r:r + n, :], src).then_inc(par_in, 16)
        act.dma_start(bf[:, :], b_fgate[0].rearrange("(h a) -> h a", a=1)).then_inc(par_in, 16)

        def split_w(u, turn=0):
            act.wait_ge(raw_in[unit(u)], turn * 16 + 16 * (u // SLOTS + 1))
            if u >= SLOTS:
                act.wait_ge(unit_used, turn * 4 + (u - SLOTS + 1))
            nc.scalar.activation(w_hi[:, unit(u), :], raw[:, unit(u), :], ACT.Copy).then_inc(w_hi_done, 1)

        for c in range(DC):
            if c == 2:
                split_w(0)
            act.wait_ge(x_tr, c + 1)
            nc.scalar.activation(a_hi[:, c, :], psum[:, 2 + c % 6, :], ACT.Copy).then_inc(x_hi_done, 1)
        split_w(1)
        for t in range(LT):
            split_w(t + 2)
            act.wait_ge(unit_used, t + 1)
            nc.scalar.activation(xb[:, t, CW - 1:], psum[:, t % 2, :], ACT.Copy).then_inc(xb_done, 1)
        for t in range(LT):
            split_w(LT + t + 2)
            act.wait_ge(unit_used, LT + t + 1)
            nc.scalar.activation(lg[:, t, :], psum[:, (LT + t) % 2, :], ACT.Gelu_apprx_tanh).then_inc(gelu_done, 1)
        act.wait_ge(gates_mm, 1)
        act.wait_ge(par_done, 1)
        for g in range(2):
            for t in range(LT):
                b = (R_BR, R_BI)[g] + t
                nc.scalar.activation(ri[:, g, t, :], psum[:, 2 + g * LT + t, :], ACT.Sigmoid,
                                     bias=par[:, b:b + 1]).then_inc(gates_done, 1)
        split_w(U_FF + 2)
        nc.scalar.activation(lam[:, 0, :], par[:, R_LAM:R_LAM + LT], ACT.Abs).then_inc(logexp_done, 1)
        act.wait_ge(logexp_done, 1)
        nc.scalar.activation(lam[:, 1, :], lam[:, 0, :], ACT.Exp, scale=-1.0).then_inc(logexp_done, 1)
        act.wait_ge(unit_used, U_FF + 1)
        act.wait_ge(par_in, 16 * PAR_DMAS)
        nc.scalar.activation(fg(0), psum[0:NFOX, U_FF % 2, :], ACT.Abs, bias=bf[:, 0:1]).then_inc(logexp_done, 1)
        act.wait_ge(logexp_done, 3)
        nc.scalar.activation(fg(1), fg(0), ACT.Exp, scale=-1.0).then_inc(logexp_done, 1)
        split_w(U_QKV + 2)
        act.wait_ge(log_decay_done, 2)
        act.wait_ge(gates_done, LT)
        for t in range(LT):
            nc.scalar.activation(a_t[:, t, :], ri[:, 0, t, :], ACT.Exp, scale=lam[:, 6, t:t + 1]).then_inc(decay_done, 1)
            nc.scalar.activation(th[:, t, :], ri[:, 0, t, :], ACT.Tanh, scale=lam[:, 7, t:t + 1]).then_inc(decay_done, 1)


        def q_high(p, u):
            act.wait_ge(unit_used, u + 1)
            nc.scalar.activation(q_hi[:, p % 2, :], psum[:, u % 2, :], ACT.Copy, scale=-SCALE).then_inc(q_hi_done, 1)

        def k_high(p, u):
            act.wait_ge(unit_used, u + 1)
            nc.scalar.activation(k_hi[:, p % 2, :], psum[:, u % 2, :], ACT.Copy).then_inc(k_hi_done, 1)

        def v_copy(p, u):
            act.wait_ge(unit_used, u + 1)
            if p >= 1:
                act.wait_ge(v_tr, p)
            nc.scalar.activation(vT[:, :], psum[:, u % 2, :], ACT.Copy).then_inc(vT_done, 1)

        def square(n):
            wait_y(act, n)
            if n >= 1:
                act.wait_ge(ms_mm, n)
            nc.scalar.activation(sq[:, :], yraw[:, n % 2, :], ACT.Square).then_inc(sq_done, 1)

        def rms(n):
            act.wait_ge(ms_mm, n + 1)
            if n >= 1:
                act.wait_ge(yn_done, n)
            nc.scalar.activation(rstd[:, :], psum[:, B_OUT, :], ACT.Ln, bias=eps[:, 0:1]).then_inc(ms_read, 1)
            act.wait_ge(ms_read, n + 1)
            nc.scalar.activation(rstd[:, :], rstd[:, :], ACT.Exp, scale=-0.5).then_inc(rstd_done, 1)

        def rstd_rows(n, s):
            k = n * ST + s
            act.wait_ge(var_done, k + 1)
            r = rstd_ln[:, s % 2:s % 2 + 1]
            nc.scalar.activation(r, mv[:, s % 2, 1:2], ACT.Ln, bias=eps[:, 1:2]).then_inc(var_log, 1)
            act.wait_ge(var_log, k + 1)
            nc.scalar.activation(r, r, ACT.Exp, scale=-0.5).then_inc(rstd_ln_done, 1)

        def y_high(n):
            act.wait_ge(yn_done, n + 1)
            act.wait_ge(unit_used, U_OUT)
            nc.scalar.activation(a_hi[:, n, :], yn[:, n, :], ACT.Copy).then_inc(y_hi_done, 1)

        def exponentials(p, i):
            for h in range(2):
                n = score_no(p, i, h)
                act.wait_ge(masked, n)
                if n > 4:
                    act.wait_ge(p_tr, n - 4)
                nc.scalar.activation(prob[:, i % 2, h, 0:(i + 1) * P], smask[:, h, 0:(i + 1) * P], ACT.Exp, scale=-1.0,
                                     bias=nmax[:, h:h + 1], accum_out=rsum[:, h:h + 1]).then_inc(exps, 1)

        def transposed_hi(p, i):
            for h in range(2):
                act.wait_ge(p_tr, score_no(p, i, h))
                if i == 0 and p >= 1:
                    act.wait_ge(pv_done, 2 * (p - 1) + h + 1)
                nc.scalar.activation(by_key(pt_hi, h, i), blocks(B_TRANS + h, i + 1), ACT.Copy).then_inc(pt_hi_done, 1)

        def attend(p, u):
            more = p + 1 < PAIRS
            if not more:
                y_high(0)
            act.wait_ge(v_tr, p + 1)
            if p >= 1:
                act.wait_ge(pv_done, 2 * p)
            nc.scalar.activation(heads(0), v_blocks(), ACT.Copy).then_inc(v_hi_done, 1)
            exponentials(p, 0)
            if p >= 1:
                values_out(p - 1)
            split_w(u + 2)
            if not more:
                y_high(1)
            exponentials(p, 1)
            transposed_hi(p, 0)
            if p == 0:
                square(0)
                act.wait_ge(consts_made, 1)
                rms(0)
            square(p + 1)
            if more:
                q_high(p + 1, u)
            else:
                y_high(2)
            exponentials(p, 2)
            transposed_hi(p, 1)
            rms(p + 1)
            split_w(u + 3)
            exponentials(p, 3)
            transposed_hi(p, 2)
            if more:
                k_high(p + 1, u + 1)
                split_w(u + 4)
            else:
                y_high(3)
            transposed_hi(p, 3)
            if more:
                v_copy(p + 1, u + 2)
        def values_out(p):
            for h in range(2):
                act.wait_ge(pv_done, 2 * p + h + 1)
                if 2 * p + h >= 1:
                    act.wait_ge(half_added, 2 * p + h)
                nc.scalar.activation(otmp[:, :], psum[DH:P, B_OUT + h, :], ACT.Copy).then_inc(o_copied, 1)

        q_high(0, U_QKV)
        act.wait_ge(root_arg, 1)
        nc.scalar.activation(th[:, :, :], th[:, :, :], ACT.Sqrt).then_inc(root_done, 1)
        split_w(U_QKV + 3)
        nc.scalar.preload_act_table_set("natural_log_exp_and_others")
        k_high(0, U_QKV + 1)
        split_w(U_QKV + 4)
        v_copy(0, U_QKV + 2)
        for p in range(PAIRS):
            attend(p, U_QKV + 3 * (p + 1))
        values_out(PAIRS - 1)
        for n in range(LT + 2, NORMS - 1):
            y_high(n)
        square(NORMS - 1)
        rms(NORMS - 1)
        y_high(NORMS - 1)
        for n in range(SLOTS, YT):
            split_w(U_OUT + n)

        def x1_high(s):
            for b in range(2):
                act.wait_ge(x1_tr, 2 * s + b + 1)
                nc.scalar.activation(a_hi[:, 4 * b:4 * b + 4, s * P:(s + 1) * P], x1_blocks(s, b), ACT.Copy)\
                  .then_inc(x1_hi_done, 1)

        rstd_rows(0, 0)
        for s in range(1, ST - 1):
            rstd_rows(0, s)
            x1_high(s - 1)
        split_w(U_FFN)
        split_w(U_FFN + 1)
        x1_high(ST - 2)
        rstd_rows(0, ST - 1)
        x1_high(ST - 1)

        def ffn_turn(it):
            for f in range(2):
                for k in range(2):
                    split_w(U_FFN + 2 + 2 * f + k, it)
                act.wait_ge(unit_used, it * 4 + (U_FFN + 2 * f + 1))
                if it is not first:
                    act.wait_ge(hid_done, it * 2 + (f - 1))
                nc.scalar.activation(silu[:, f, :], psum[:, 2 * f, :], ACT.Silu).then_inc(silu_done, 1)

        first = 0
        ffn_turn(first)
        with act.Fori(1, FT // 2) as it:
            ffn_turn(it)

        def split_h(f, turn=0):
            if f >= SLOTS:
                act.wait_ge(unit_used, turn * 4 + (U_DOWN + f - SLOTS + 1))
            act.wait_ge(hid_done, turn * 4 + (f + 1))
            nc.scalar.activation(h_hi[:, f % SLOTS, :], hid[:, bass.ds(turn * (4 * S) + f * S, S)], ACT.Copy)\
              .then_inc(h_hi_done, 1)

        split_h(0)
        split_h(1)
        for f in range(2, 4):
            split_w(U_DOWN + f)
            split_h(f)
        with act.Fori(0, DOWN_TURNS) as it:
            for f in range(4, 8):
                split_w(U_DOWN + f, it)
                split_h(f, it)
        for f in range(FT - 2, FT):
            split_w(U_DOWN + f)
            split_h(f)
        nc.scalar.preload_act_table_set("natural_log_exp_and_others")
        for s in range(ST):
            rstd_rows(1, s)
        act.wait_ge(out_ready, 2 * ST)
        act.dma_start(out_v[:, ST - 1, BN:], z[:, (ST - 1) % 2, BN:]).then_inc(out_stored[(ST - 1) % 2], 16)

    @block.vector
    def _(dve):
        steps = [0]

        def step(ins):
            steps[0] += 1
            ins.then_inc(dve_step, 1)
            return steps[0]

        def settled(n=None):
            dve.wait_ge(dve_step, n or steps[0])

        def split_w(u, turn=0):
            dve.wait_ge(w_hi_done, turn * 4 + (u + 1))
            nc.vector.tensor_tensor(w_lo[:, unit(u), :], raw[:, unit(u), :], f32(w_hi[:, unit(u), :]), ALU.subtract)\
              .then_inc(w_lo_done, 1)

        def log_sigmoid(t):
            step(nc.vector.tensor_scalar(t(3), t(1), 2.0, None, ALU.add))
            settled()
            step(nc.vector.reciprocal(t(4), t(3)))
            settled()
            step(nc.vector.tensor_tensor(t(3), t(1), t(4), ALU.mult))
            settled()
            step(nc.vector.tensor_tensor(t(4), t(3), t(3), ALU.mult))
            settled()
            step(nc.vector.tensor_scalar(t(5), t(4), ATANH[-1], None, ALU.mult))
            for c in reversed(ATANH[:-1]):
                settled()
                step(nc.vector.scalar_tensor_tensor(t(5), t(5), c, t(4), ALU.add, ALU.mult))
            settled()
            step(nc.vector.scalar_tensor_tensor(t(5), t(5), 1.0, t(3), ALU.add, ALU.mult))
            settled()
            step(nc.vector.scalar_tensor_tensor(t(0), t(5), -2.0, t(2), ALU.mult, ALU.add))
            settled()

        def q_low(p, u):
            dve.wait_ge(q_hi_done, p + 1)
            nc.vector.scalar_tensor_tensor(q_lo[:, p % 2, :], psum[:, u % 2, :], -SCALE, f32(q_hi[:, p % 2, :]),
                                           ALU.mult, ALU.subtract).then_inc(q_lo_done, 1)

        def k_low(p, u):
            dve.wait_ge(k_hi_done, p + 1)
            nc.vector.tensor_tensor(k_lo[:, p % 2, :], psum[:, u % 2, :], f32(k_hi[:, p % 2, :]), ALU.subtract)\
              .then_inc(k_lo_done, 1)

        for c in range(DC):
            if c == 2:
                split_w(0)
            dve.wait_ge(x_hi_done, c + 1)
            nc.vector.tensor_tensor(a_lo[:, c, :], psum[:, 2 + c % 6, :], f32(a_hi[:, c, :]), ALU.subtract)\
              .then_inc(x_lo_done, 1)
        split_w(1)
        dve.wait_ge(par_tr, 1)
        nc.vector.tensor_copy(par[:, 0:NPAR], psum[:, 7, 0:NPAR]).then_inc(par_done, 1)
        dve.wait_ge(par_done, 1)
        for t in range(LT):
            split_w(t + 2)
            dve.wait_ge(xb_done, t + 1)
            dve.wait_ge(pad_made, 1)

            def tap(j):
                n = R_CONV + j * LT + t
                return xb[:, t, j:j + S], par[:, n:n + 1]

            src, w = tap(CW - 1)
            step(nc.vector.tensor_scalar(xc[:, t, :], src, w, par[:, R_CONVB + t:R_CONVB + t + 1], ALU.mult, ALU.add))
            for j in reversed(range(CW - 1)):
                src, w = tap(j)
                settled()
                ins = nc.vector.scalar_tensor_tensor(xc[:, t, :], src, w, xc[:, t, :], ALU.mult, ALU.add)
                if j:
                    step(ins)
            ins.then_inc(conv_done, 1)
        split_w(LT + 2)
        split_w(LT + 3)
        split_w(LT + 4)
        dve.wait_ge(logexp_done, 2)
        step(nc.vector.tensor_scalar(lam[:, 2, :], par[:, R_LAM:R_LAM + LT], 0.0, None, ALU.min))
        log_sigmoid(lambda k: lam[:, k, :])
        for k, sign in ((6, 1.0), (7, -1.0)):
            nc.vector.tensor_scalar(lam[:, k, :], lam[:, 0, :], sign * LRU_C, None, ALU.mult).then_inc(log_decay_done, 1)
        dve.wait_ge(logexp_done, 4)
        nc.vector.tensor_scalar(fg(2), psum[0:NFOX, U_FF % 2, :], bf[:, 0:1], 0.0, ALU.add, ALU.min)\
          .then_inc(ff_read, 1)
        split_w(U_QKV + 2)
        q_low(0, U_QKV)
        dve.wait_ge(decay_done, 2 * LT)
        dve.wait_ge(gates_done, 2 * LT)
        sq_a = xb[:, :, 0:S]
        step(nc.vector.tensor_tensor(sq_a, a_t[:, :, :], a_t[:, :, :], ALU.mult))
        settled()
        step(nc.vector.scalar_tensor_tensor(th[:, :, :], sq_a, 1.0, th[:, :, :], ALU.add, ALU.mult))
        settled()
        nc.vector.tensor_scalar(th[:, :, :], th[:, :, :], 1e-32, None, ALU.max).then_inc(root_arg, 1)
        split_w(U_QKV + 3)
        step(nc.vector.tensor_tensor(xc[:, :, :], ri[:, 1, :, :], xc[:, :, :], ALU.mult))
        settled()
        k_low(0, U_QKV + 1)
        dve.wait_ge(root_done, 1)
        step(nc.vector.tensor_tensor(th[:, :, :], th[:, :, :], xc[:, :, :], ALU.mult))
        settled()
        for t in range(LT):
            step(nc.vector.tensor_tensor_scan(xb[:, t, 0:S], a_t[:, t, :], th[:, t, :], 0.0, ALU.mult, ALU.add))
        dve.wait_ge(gelu_done, LT)
        settled()
        for t in range(LT):
            nc.vector.tensor_tensor(yraw[:, t, :], xb[:, t, 0:S], lg[:, t, :], ALU.mult).then_inc(lru_done, 1)

        def norm(n):
            dve.wait_ge(rstd_done, n + 1)
            g = R_G + y_tile[n]
            nc.vector.scalar_tensor_tensor(yn[:, n, :], yraw[:, n % 2, :], par[:, g:g + 1], rstd[:, :],
                                           ALU.mult, ALU.mult).then_inc(yn_done, 1)

        def y_low(n):
            dve.wait_ge(y_hi_done, n + 1)
            nc.vector.tensor_tensor(a_lo[:, n, :], yn[:, n, :], f32(a_hi[:, n, :]), ALU.subtract).then_inc(y_lo_done, 1)

        def mask_scores(p, i):
            w = (i + 1) * P
            for h in range(2):
                n = score_no(p, i, h)
                dve.wait_ge(scores, n)
                if n > 2:
                    dve.wait_ge(exps, n - 2)
                nc.vector.tensor_tensor_reduce(out=smask[:, h, 0:w], in0=psum[:, B_SCORE + h, 0:w], in1=mask[:, S - w:S],
                                               scale=1.0, scalar=BIG, op0=ALU.add, op1=ALU.min,
                                               accum_out=nmax[:, h:h + 1]).then_inc(masked, 1)

        def normalise(p, i):
            for h in range(2):
                dve.wait_ge(exps, score_no(p, i, h))
                step(nc.vector.reciprocal(rinv[:, h:h + 1], rsum[:, h:h + 1]))
            for h in range(2):
                settled()
                row = prob[:, i % 2, h, 0:(i + 1) * P]
                nc.vector.tensor_scalar(row, row, rinv[:, h:h + 1], None, ALU.mult).then_inc(probs, 1)

        def transposed_lo(p, i):
            for h in range(2):
                dve.wait_ge(pt_hi_done, score_no(p, i, h))
                nc.vector.tensor_tensor(by_key(pt_lo, h, i), blocks(B_TRANS + h, i + 1), f32(by_key(pt_hi, h, i)),
                                        ALU.subtract).then_inc(pt_lo_done, 1)

        def attend(p, u):
            more = p + 1 < PAIRS
            if not more:
                y_low(0)
            mask_scores(p, 0)
            dve.wait_ge(v_hi_done, p + 1)
            nc.vector.tensor_tensor(heads(1), v_blocks(), f32(heads(0)), ALU.subtract).then_inc(v_lo_done, 1)
            normalise(p, 0)
            mask_scores(p, 1)
            if p >= 1:
                values_sum(p - 1)
            if not more:
                y_low(1)
            else:
                split_w(u + 2)
            normalise(p, 1)
            transposed_lo(p, 0)
            if not more:
                split_w(u + 2)
            if p == 0:
                norm(0)
            if p == MOBAP - 1:
                dve.wait_ge(forget_log, 1)
                nc.vector.tensor_tensor_scan(fg(1), f32(fox_g[0:NFOX, :]), fg(0), 0.0, ALU.mult, ALU.add)\
                  .then_inc(forget_sum, 1)
            mask_scores(p, 2)
            if more:
                q_low(p + 1, u)
            else:
                y_low(2)
            transposed_lo(p, 1)
            normalise(p, 2)
            mask_scores(p, 3)
            if more:
                norm(p + 1)
                split_w(u + 3)
            normalise(p, 3)
            transposed_lo(p, 2)
            if not more:
                split_w(u + 3)
                norm(p + 1)
            if more:
                k_low(p + 1, u + 1)
                split_w(u + 4)
            else:
                y_low(3)
            transposed_lo(p, 3)
        def values_sum(p):
            for h in range(2):
                dve.wait_ge(o_copied, 2 * p + h + 1)
                nc.vector.tensor_tensor(yraw[h * DH:(h + 1) * DH, (p + LT) % 2, :], psum[0:DH, B_OUT + h, :],
                                        otmp[:, :], ALU.add).then_inc(half_added, 1)

        split_w(U_QKV + 4)
        dve.wait_ge(consts_made, 1)
        for p in range(PAIRS):
            attend(p, U_QKV + 3 * (p + 1))
        values_sum(PAIRS - 1)
        for n in range(LT + 2, NORMS - 1):
            y_low(n)
        norm(NORMS - 1)
        y_low(NORMS - 1)
        for n in range(SLOTS, YT):
            split_w(U_OUT + n)

        def layer_norm(n, s, dst, summed, done, between=None):
            k = n * ST + s
            m = mv[:, s % 2, :]
            var, root, t = m[:, 1:2], rstd_ln[:, s % 2:s % 2 + 1], root_t[:, s % 2, :]
            half = [slice(b * BN, (b + 1) * BN) for b in range(2)]
            zs = [z[:, s % 2, half[b]] for b in range(2)]
            for b in range(2):
                dve.wait_ge(summed, 2 * s + b + 1)
                settled(step(nc.vector.scalar_tensor_tensor(zs[b], x_nat[:, s, half[b]], ALPHA, psum[:, 2 * s + b, :],
                                                            ALU.mult, ALU.add)))
                step(nc.vector.bn_stats(stats[:, s % 2, b, :], zs[b]))
            settled()
            nc.vector.bn_aggr(m, stats[:, s % 2, :, :].rearrange("p b k -> p (b k)")).then_inc(var_done, 1)
            dve.wait_ge(var_done, k + 1)
            shifted = step(nc.vector.tensor_scalar(t[:, 0:1], var, LN_EPS, None, ALU.add))
            scaled = [step(nc.vector.scalar_tensor_tensor(zs[0], zs[0], m[:, 0:1], gb[:, 0, half[0]],
                                                          ALU.subtract, ALU.mult))]
            dve.wait_ge(rstd_ln_done, k + 1)
            settled(shifted)
            a = step(nc.vector.scalar_tensor_tensor(t[:, 1:2], t[:, 0:1], root, root, ALU.mult, ALU.mult))
            if between and s == ST - 1:
                between()
            scaled.append(step(nc.vector.scalar_tensor_tensor(zs[1], zs[1], m[:, 0:1], gb[:, 0, half[1]],
                                                              ALU.subtract, ALU.mult)))
            settled(a)
            settled(step(nc.vector.tensor_scalar(t[:, 2:3], t[:, 1:2], -0.5, 1.5, ALU.mult, ALU.add)))
            settled(step(nc.vector.tensor_tensor(t[:, 3:4], t[:, 2:3], root, ALU.mult)))
            for b in range(2):
                settled(scaled[b])
                nc.vector.scalar_tensor_tensor(dst[:, half[b]], zs[b], t[:, 3:4], gb[:, 1, half[b]],
                                               ALU.mult, ALU.add).then_inc(done, 1)
            if between and s < ST - 1:
                between()

        def x1_low(s):
            for b in range(2):
                dve.wait_ge(x1_hi_done, 2 * s + b + 1)
                cols = slice(s * P, (s + 1) * P)
                nc.vector.tensor_tensor(a_lo[:, 4 * b:4 * b + 4, cols], x1_blocks(s, b),
                                        f32(a_hi[:, 4 * b:4 * b + 4, cols]), ALU.subtract).then_inc(x1_lo_done, 1)

        dve.wait_ge(gb_in, 32)
        for s in range(ST):
            layer_norm(0, s, x_nat[:, s, :], rows_mixed, x1_done, (lambda: x1_low(s - 1)) if s >= 1 else None)
        x1_low(ST - 1)
        dve.wait_ge(w_lo_done, U_FFN + 2)

        def ffn_turn(it):
            for f in range(2):
                for k in range(2):
                    split_w(U_FFN + 2 + 2 * f + k, it)
                dve.wait_ge(silu_done, it * 2 + (f + 1))
                dve.wait_ge(unit_used, it * 4 + (U_FFN + 2 * f + 2))
                nc.vector.tensor_tensor(hid[:, bass.ds(it * (2 * S) + f * S, S)], psum[:, 2 * f + 1, :], silu[:, f, :],
                                        ALU.mult).then_inc(hid_done, 1)

        ffn_turn(0)
        with dve.Fori(1, FT // 2) as it:
            ffn_turn(it)

        def split_h(f, turn=0):
            dve.wait_ge(h_hi_done, turn * 4 + (f + 1))
            nc.vector.tensor_tensor(h_lo[:, f % SLOTS, :], hid[:, bass.ds(turn * (4 * S) + f * S, S)],
                                    f32(h_hi[:, f % SLOTS, :]), ALU.subtract).then_inc(h_lo_done, 1)

        split_h(0)
        split_h(1)
        for f in range(2, 4):
            split_w(U_DOWN + f)
            split_h(f)
        with dve.Fori(0, DOWN_TURNS) as it:
            for f in range(4, 8):
                split_w(U_DOWN + f, it)
                split_h(f, it)
        for f in range(FT - 2, FT):
            split_w(U_DOWN + f)
            split_h(f)
        dve.wait_ge(gb_in, 64)
        for s in range(ST):
            if s >= 2:
                dve.wait_ge(out_stored[s % 2], 32 * (s // 2))
            layer_norm(1, s, z[:, s % 2, :], rows_down, out_ready)

    @block.tensor
    def _(pe):
        def three(dst, s_hi, s_lo, m_hi, m_lo, start, stop):
            nc.tensor.matmul(dst, s_hi, m_hi, start=start, stop=False)
            nc.tensor.matmul(dst, s_hi, m_lo, start=False, stop=False)
            return nc.tensor.matmul(dst, s_lo, m_hi, start=False, stop=stop)

        def unit_ready(u, turn=0):
            pe.wait_ge(w_lo_done, turn * 4 + (u + 1))

        def chunk(dst, u, c, rows=slice(0, S)):
            cols = slice(c * P, (c + 1) * P)
            return three(dst, w_hi[:, unit(u), cols], w_lo[:, unit(u), cols], a_hi[:, c, rows], a_lo[:, c, rows],
                         c == 0, c == DC - 1)

        def bank_free(u):
            v = u - 2
            if 0 <= v < LT:
                pe.wait_ge(xb_done, v + 1)
            elif LT <= v < 2 * LT:
                pe.wait_ge(gelu_done, v - LT + 1)
            elif v == U_FF:
                pe.wait_ge(ff_read, 1)
            elif v > U_FF:
                p, k = divmod(v - U_QKV, 3)
                pe.wait_ge((q_lo_done, k_lo_done, vT_done)[k], p + 1)

        def project(u, quarter):
            if quarter == 0:
                unit_ready(u)
                bank_free(u)
            for c in range(2 * quarter, 2 * quarter + 2):
                if u == 0:
                    pe.wait_ge(x_lo_done, c + 1)
                last = chunk(psum[:, u % 2, :], u, c)
            if quarter == 3:
                last.then_inc(unit_used, 1)

        def gates():
            pe.wait_ge(conv_done, LT)
            pe.wait_ge(gate_in, 16 * 4 * LT)
            for g in range(2):
                for t in range(LT):
                    last = nc.tensor.matmul(psum[:, 2 + g * LT + t, :], gate_w[:, g * LT + t, :], xc[:, t, :],
                                            start=True, stop=True)
            last.then_inc(gates_mm, 1)

        def mean_square(n):
            pe.wait_ge(sq_done, n + 1)
            if n >= 1:
                pe.wait_ge(ms_read, n)
            nc.tensor.matmul(psum[:, B_OUT, :], blockmean[:, :], sq[:, :], start=True, stop=True).then_inc(ms_mm, 1)

        def transpose_v(p):
            pe.wait_ge(vT_done, p + 1)
            if p >= 1:
                pe.wait_ge(pt_lo_done, score_no(p - 1, ST - 1, 0))
            for t in range(ST):
                last = nc.tensor.transpose(psum[:, B_TRANS, t * P:(t + 1) * P], vT[:, t * P:(t + 1) * P], ident[:, :])
            last.then_inc(v_tr, 1)

        def score(p, i):
            w = (i + 1) * P
            if i == 0:
                pe.wait_ge(q_lo_done, p + 1)
                pe.wait_ge(k_lo_done, p + 1)
            for h in range(2):
                n = score_no(p, i, h)
                if n > 2:
                    pe.wait_ge(masked, n - 2)
                dst = psum[:, B_SCORE + h, 0:w]
                rows = slice(h * DH, (h + 1) * DH)
                cols = slice(i * P, (i + 1) * P)
                fox = p >= MOBAP
                if fox:
                    pe.wait_ge(fox_q_done, 2 * (p - MOBAP) + h + 1)
                    nc.tensor.matmul(dst, fox_q[:, h, cols], fox_k[:, 0:w], start=True, stop=False)
                b = p % 2
                three(dst, q_hi[rows, b, cols], q_lo[rows, b, cols], k_hi[rows, b, 0:w], k_lo[rows, b, 0:w],
                      not fox, True).then_inc(scores, 1)

        def transpose_p(p, i):
            for h in range(2):
                n = score_no(p, i, h)
                pe.wait_ge(probs, n)
                if n > 2:
                    pe.wait_ge(pt_lo_done, n - 2)
                if i == 0 and h == 0:
                    pe.wait_ge(v_lo_done, p + 1)
                for j in range(i + 1):
                    last = nc.tensor.transpose(psum[:, B_TRANS + h, j * P:(j + 1) * P],
                                               prob[:, i % 2, h, j * P:(j + 1) * P], ident[:, :])
                last.then_inc(p_tr, 1)

        def values(p, h):
            pe.wait_ge(pt_lo_done, score_no(p, ST - 1, h))
            pe.wait_ge(ms_read, p + 2)
            if p >= 1:
                pe.wait_ge(half_added, 2 * (p - 1) + h + 1)
            for j in range(ST):
                cols = slice(j * PT_STRIDE + j * P, j * PT_STRIDE + S)
                for buf in (pt_hi, pt_lo):
                    last = nc.tensor.matmul(psum[:, B_OUT + h, j * P:S], vv[:, j, h, :], buf[:, h, cols],
                                            start=(j == 0 and buf is pt_hi), stop=(j == ST - 1 and buf is pt_lo))
            last.then_inc(pv_done, 1)

        def rows_times(s, a_parts, w_slot, first, last_one, only=None):
            hi, lo = (a[:, s * P:(s + 1) * P] for a in a_parts)
            steps = [(hi, w_hi, 0), (hi, w_hi, 1), (hi, w_lo, 0), (hi, w_lo, 1), (lo, w_hi, 0), (lo, w_hi, 1)]
            for k in (only if only is not None else range(6)):
                a, w, half = steps[k]
                last = nc.tensor.matmul(psum[:, 2 * s + half, :], a, w[:, w_slot, half * S:(half + 1) * S],
                                        start=first and k < 2, stop=last_one and k >= 4)
            return last

        HALF = [(0, 2, 4), (1, 3, 5)]

        def mix_rows(s, n, only=None):
            if s == 0 or n >= SLOTS:
                unit_ready(U_OUT + n)
                pe.wait_ge(y_lo_done, n + 1)
            return rows_times(s, (a_hi[:, n, :], a_lo[:, n, :]), unit(U_OUT + n), n == 0, n == YT - 1, only)

        def attend(p, beside):
            take = iter(beside)

            def piece(n=1):
                for _ in range(n):
                    next(take)()

            if p + 1 < PAIRS:
                piece()
                transpose_v(p)
                score(p, 0)
                piece()
            else:
                transpose_v(p)
                score(p, 0)
                piece(2)
            score(p, 1)
            piece()
            transpose_p(p, 0)
            piece()
            if p == 0:
                mean_square(0)
            score(p, 2)
            piece()
            transpose_p(p, 1)
            mean_square(p + 1)
            piece()
            score(p, 3)
            transpose_p(p, 2)
            piece(3)
            transpose_p(p, 3)
            piece()
            values(p, 0)
            piece()
            values(p, 1)
            piece()

        pe.wait_ge(ident_made, 1)
        for c in range(DC):
            pe.wait_ge(x_in[c * ST // DC], 16)
            if c >= 6:
                pe.wait_ge(x_lo_done, c - 5)
            for t in range(ST):
                last = nc.tensor.transpose(psum[:, 2 + c % 6, t * P:(t + 1) * P], x_nat[:, t, c * P:(c + 1) * P],
                                           ident[:, :])
            last.then_inc(x_tr, 1)
        for u in range(U_FF):
            for quarter in range(4):
                project(u, quarter)
            if u == 0:
                pe.wait_ge(par_in, 16 * PAR_DMAS)
                pe.wait_ge(x_lo_done, DC)
                nc.tensor.transpose(psum[:, 7, 0:NPAR], par_rows[0:NPAR, :], ident[0:NPAR, 0:NPAR]).then_inc(par_tr, 1)
            if u == U_FF - 2:
                gates()
        for u in range(U_FF, U_QKV + 3):
            for quarter in range(4):
                project(u, quarter)
        pe.wait_ge(gates_done, 2 * LT)
        for p in range(PAIRS):
            u = U_QKV + 3 * (p + 1)
            if p + 1 < PAIRS:
                beside = [(lambda v=u + k // 4, q=k % 4: project(v, q)) for k in range(12)]
            else:
                beside = [(lambda n=k // 3, t=k % 3: mix_rows(0, n, (2 * t, 2 * t + 1))) for k in range(12)]
            attend(p, beside)
        pe.wait_ge(masked, score_no(PAIRS - 1, ST - 1, 1))
        for n in range(SLOTS):
            mix_rows(1, n)
        mean_square(NORMS - 1)
        pe.wait_ge(pt_lo_done, score_no(PAIRS - 1, ST - 1, 1))
        for n in range(SLOTS):
            mix_rows(2, n)
        pe.wait_ge(ms_read, NORMS)
        for n in range(SLOTS):
            mix_rows(3, n).then_inc(unit_used, 1)

        def transpose_x1(s):
            for c in range(DC):
                if c % 4 == 0:
                    pe.wait_ge(x1_done, 2 * s + c // 4 + 1)
                last = nc.tensor.transpose(psum[:, 2 * s + c // 4, (c % 4) * P:(c % 4 + 1) * P],
                                           x_nat[:, s, c * P:(c + 1) * P], ident[:, :])
                if c % 4 == 3:
                    last.then_inc(x1_tr, 1)
                elif c == 0 and s == ST - 2:
                    last.then_inc(unit_used, 1)

        for s in range(ST):
            for b in range(2):
                for n in range(SLOTS, YT):
                    last = mix_rows(s, n, HALF[b])
                    if s == ST - 1 and b == 1 and n < YT - 1:
                        last.then_inc(unit_used, 1)
                last.then_inc(rows_mixed, 1)
            if s >= 1:
                transpose_x1(s - 1)

        for rows in range(2):
            for k in range(2):
                pe.wait_ge(x1_lo_done, 4 * (rows + 1))
                unit_ready(U_FFN + k)
                for c in range(DC):
                    last = chunk(psum[:, k, rows * (S // 2):(rows + 1) * (S // 2)], U_FFN + k, c,
                                 slice(rows * (S // 2), (rows + 1) * (S // 2)))
                if rows == 1:
                    last.then_inc(unit_used, 1)
            if rows == 0:
                transpose_x1(ST - 1)

        def ffn_turn(it, units=range(4)):
            for k in units:
                unit_ready(U_FFN + k, it)
                if it is not first:
                    pe.wait_ge((silu_done, hid_done)[k % 2], it * 2 + (k // 2 - 1))
                for c in range(DC):
                    last = chunk(psum[:, k, :], U_FFN + k, c)
                last.then_inc(unit_used, 1)

        first = 0
        ffn_turn(first, range(2, 4))
        with pe.Fori(1, FT // 2) as it:
            ffn_turn(it)

        pe.wait_ge(silu_done, FT)
        pe.wait_ge(hid_done, FT)

        def down(f, s, only=None):
            return rows_times(s, (h_hi[:, f % SLOTS, :], h_lo[:, f % SLOTS, :]), unit(U_DOWN + f),
                              f == 0, f == FT - 1, only)

        def down_ready(f, turn=0):
            unit_ready(U_DOWN + f, turn)
            pe.wait_ge(h_lo_done, turn * 4 + (f + 1))

        for f in range(2):
            down_ready(f)
            for s in range(ST):
                last = down(f, s)
            last.then_inc(unit_used, 1)
        with pe.Fori(0, DOWN_TURNS) as it:
            for f in range(2, 6):
                down_ready(f, it)
                for s in range(ST):
                    last = down(f, s)
                last.then_inc(unit_used, 1)
        for s in range(ST):
            for b in range(2):
                for f in range(FT - 4, FT):
                    if s == 0 and b == 0:
                        down_ready(f)
                    last = down(f, s, HALF[b])
                last.then_inc(rows_down, 1)

    ctx.close()


_INS = ['x', 'w_in', 'b_fgate', 'conv_w', 'conv_b', 'w_rgate', 'b_rgate', 'w_igate', 'b_igate', 'lru_lambda',
        'out_norm_g', 'w_out', 'ln1_g', 'ln1_b', 'w_ffn_gate', 'w_ffn_up', 'w_ffn_down', 'ln2_g', 'ln2_b']


def kernel(**inputs):
    import numpy as np
    import concourse.bacc as bacc
    from concourse.bass_utils import run_bass_kernel_spmd

    nc = bacc.Bacc("TRN2", target_bir_lowering=False, num_devices=1)
    arrays, args = {}, []
    for name in _INS:
        a = np.ascontiguousarray(inputs[name])
        arrays[f"in_{name}_dram"] = a
        args.append(nc.dram_tensor(f"in_{name}_dram", a.shape, mybir.dt.from_np(a.dtype), kind="ExternalInput").ap())
    shape = np.shape(inputs['x'])
    args.append(nc.dram_tensor("out_0_dram", shape, mybir.dt.float32, kind="ExternalOutput").ap())
    hymba_layer(nc, *args)
    r = run_bass_kernel_spmd(nc, [arrays], core_ids=[0])
    return r.results[0]["out_0_dram"]
```

```python
import math
from contextlib import ExitStack

import concourse.bass as bass
from concourse import mybir



def hymba_layer(nc, x, w_in, b_fgate, conv_w, conv_b, w_rgate, b_rgate, w_igate, b_igate, lru_lambda,
                out_norm_g, w_out, ln1_g, ln1_b, w_ffn_gate, w_ffn_up, w_ffn_down, ln2_g, ln2_b, out):
    F32 = mybir.dt.float32
    F32R = mybir.dt.float32r
    ALU = mybir.AluOpType
    ACT = mybir.ActivationFunctionType

    P = 128
    _, S, D = x.shape
    DC = D // P
    ST = S // P
    NFOX = b_fgate.shape[1]
    DH = w_rgate.shape[2]
    DLRU = conv_b.shape[1]
    DFOX = NFOX * DH
    DMOBA = D - DLRU - DFOX
    F = w_ffn_gate.shape[2]
    FT = F // P
    CW = conv_w.shape[1]
    PAIRS = (DFOX + DMOBA) // P
    FOXP = DFOX // P
    MOBAP = DMOBA // P
    LT = DLRU // P
    YT = D // P
    ALPHA = 2 ** 0.25
    SCALE = 1.0 / math.sqrt(DH)
    BIG = 1e30
    LRU_C = 8.0
    LN_EPS = 1e-5
    RMS_EPS = 1e-6
    BN = 512

    C_FQ, C_FK, C_FV, C_FF = 0, DFOX, 2 * DFOX, 3 * DFOX
    C_MQ = C_FF + NFOX
    C_MK = C_MQ + DMOBA
    C_MV = C_MK + DMOBA
    C_LX = C_MV + DMOBA
    C_LG = C_LX + DLRU

    U_FF = 2 * LT
    U_QKV = U_FF + 1
    U_OUT = U_QKV + 3 * PAIRS
    U_FFN = U_OUT + YT
    U_DOWN = U_FFN + 2 * FT
    SLOTS = 4
    proj_col = [C_LX + P * t for t in range(LT)] + [C_LG + P * t for t in range(LT)] + [C_FF]
    for p in range(MOBAP):
        proj_col += [C_MQ + P * p, C_MK + P * p, C_MV + P * p]
    for p in range(FOXP):
        proj_col += [C_FQ + P * p, C_FK + P * p, C_FV + P * p]
    y_tile = [FOXP + MOBAP + t for t in range(LT)]
    y_tile += [FOXP + p for p in range(MOBAP)] + [p for p in range(FOXP)]

    assert max(-(-S // 256), 3) == 3

    ctx = ExitStack()
    common = ctx.enter_context(ExitStack())

    def sb(stack, name, shape, dt=F32):
        return stack.enter_context(nc.sbuf_tensor(name, shape, dt))

    def sem(name):
        return ctx.enter_context(nc.semaphore(name))

    raw = sb(common, "raw", [P, SLOTS, D])
    w_hi = sb(common, "w_hi", [P, SLOTS, D], F32R)
    w_lo = sb(common, "w_lo", [P, SLOTS, D], F32R)
    a_hi = sb(common, "a_hi", [P, DC, S], F32R)
    a_lo = sb(common, "a_lo", [P, DC, S], F32R)
    x_nat = sb(common, "x_nat", [P, ST, D])
    gb = sb(common, "gb", [P, 2, D])
    ident = sb(common, "ident", [P, P])
    stats = sb(common, "stats", [P, 2, D // BN, 6])
    mv = sb(common, "mv", [P, 2, 2])
    eps = sb(common, "eps", [P, 2])
    rstd_ln = sb(common, "rstd_ln", [P, 2])
    root_t = sb(common, "root_t", [P, 2, 3])

    mix = ExitStack()
    qq = sb(mix, "qq", [P, 2, 2, S], F32R)
    kk = sb(mix, "kk", [P, 2, 2, S], F32R)
    k_lo = sb(mix, "k_lo", [P, 2, S], F32R)
    vT = sb(mix, "vT", [P, S])
    vv = sb(mix, "vv", [P, ST, 2, 2 * DH], F32R)
    yraw = sb(mix, "yraw", [P, 2, S])
    otmp = sb(mix, "otmp", [DH, 2, S])
    sq = sb(mix, "sq", [P, S])
    log_ms = sb(mix, "log_ms", [P, ST * 2])
    rstd = sb(mix, "rstd", [P, ST * 2, DH])
    yn = sb(mix, "yn", [P, YT, S])
    mask = sb(mix, "mask", [P, S])
    headmean = sb(mix, "headmean", [P, 2])
    par_rows = sb(mix, "par_rows", [P, P])
    par = sb(mix, "par", [P, 32])
    lam = sb(mix, "lam", [P, 8, LT])
    fox_q = sb(mix, "fox_q", [P, 2, S], F32R)
    fox_g = sb(mix, "fox_g", [P, S], F32R)
    fox_k = sb(mix, "fox_k", [P, S], F32R)
    onehot = sb(mix, "onehot", [P, NFOX])
    bf = sb(mix, "bf", [NFOX, 1])
    nmax = sb(mix, "nmax", [P, 2])
    rsum = sb(mix, "rsum", [P, 2])
    rinv = sb(mix, "rinv", [P, 2])

    lru = ExitStack()
    xb = sb(lru, "xb", [P, LT, CW - 1 + S])
    ri = sb(lru, "ri", [P, 2, LT, S])
    xc = sb(lru, "xc", [P, LT, S])
    a_t = sb(lru, "a_t", [P, LT, S])
    th = sb(lru, "th", [P, LT, S])
    gate_w = sb(lru, "gate_w", [P, 2 * LT, P])
    lru.close()
    att = ExitStack()
    PT_STRIDE = S - P
    PT_COLS = (ST - 1) * PT_STRIDE + S
    pt_hi = sb(att, "pt_hi", [P, 2, PT_COLS], F32R)
    pt_lo = sb(att, "pt_lo", [P, 2, PT_COLS], F32R)
    smask = sb(att, "smask", [P, 2, S])
    prob = sb(att, "prob", [P, 2, 2, S])
    att.close()
    mix.close()

    ffn = ExitStack()
    hid = sb(ffn, "hid", [P, FT * S])
    h_hi = sb(ffn, "h_hi", [P, SLOTS, S], F32R)
    h_lo = sb(ffn, "h_lo", [P, SLOTS, S], F32R)
    silu = sb(ffn, "silu", [P, 2, S])
    z = sb(ffn, "z", [P, 2, D])
    ffn.close()

    lg = yn[:, YT - 2 - LT:YT - 2, :]

    def fg(k):
        return gb[0:NFOX, k // 2, k % 2 * S:(k % 2 + 1) * S] if k < 4 else yn[0:NFOX, YT + 3 - k, :]


    psum = ctx.enter_context(nc.psum_tensor("psum", [P, 8, S], F32))
    B_SCORE, B_TRANS, B_OUT = 2, 4, 6

    x_in = [sem(f"x_in{g}") for g in range(ST)]
    raw_in = [sem(f"raw_in{i}") for i in range(SLOTS)]
    par_in = sem("par_in")
    gate_in = sem("gate_in")
    gb_in = sem("gb_in")
    pad_made = sem("pad_made")
    ident_made = sem("ident_made")
    consts_made = sem("consts_made")
    pool_step = sem("pool_step")
    x_tr = sem("x_tr")
    x_hi_done = sem("x_hi_done")
    x_lo_done = sem("x_lo_done")
    w_hi_done = sem("w_hi_done")
    w_lo_done = sem("w_lo_done")
    unit_used = sem("unit_used")
    par_tr = sem("par_tr")
    par_done = sem("par_done")
    xb_done = sem("xb_done")
    conv_done = sem("conv_done")
    gates_mm = sem("gates_mm")
    gates_done = sem("gates_done")
    gelu_done = sem("gelu_done")
    decay_done = sem("decay_done")
    logexp_done = sem("logexp_done")
    log_decay_done = sem("log_decay_done")
    ff_read = sem("ff_read")
    forget_log = sem("forget_log")
    forget_sum = sem("forget_sum")
    fox_ready = sem("fox_ready")
    fox_q_done = sem("fox_q_done")
    lru_done = sem("lru_done")
    sq_done = sem("sq_done")
    ms_mm = sem("ms_mm")
    ms_read = sem("ms_read")
    rstd_spread = sem("rstd_spread")
    yn_done = sem("yn_done")
    q_hi_done = sem("q_hi_done")
    k_hi_done = sem("k_hi_done")
    q_lo_done = sem("q_lo_done")
    k_lo_done = sem("k_lo_done")
    k_copied = sem("k_copied")
    vT_done = sem("vT_done")
    v_tr = sem("v_tr")
    v_hi_done = sem("v_hi_done")
    v_lo_done = sem("v_lo_done")
    scores = sem("scores")
    masked = sem("masked")
    exps = sem("exps")
    probs = sem("probs")
    p_tr = sem("p_tr")
    pt_hi_done = sem("pt_hi_done")
    pt_lo_done = sem("pt_lo_done")
    pv_done = sem("pv_done")
    o_copied = sem("o_copied")
    half_added = sem("half_added")
    y_hi_done = sem("y_hi_done")
    y_lo_done = sem("y_lo_done")
    rows_mixed = sem("rows_mixed")
    x1_done = sem("x1_done")
    x1_tr = sem("x1_tr")
    x1_hi_done = sem("x1_hi_done")
    x1_lo_done = sem("x1_lo_done")
    silu_done = sem("silu_done")
    hid_done = sem("hid_done")
    h_hi_done = sem("h_hi_done")
    h_lo_done = sem("h_lo_done")
    root_arg = sem("root_arg")
    root_done = sem("root_done")
    rstd_done = sem("rstd_done")
    var_done = sem("var_done")
    var_log = sem("var_log")
    rstd_ln_done = sem("rstd_ln_done")
    root_refined = sem("root_refined")
    out_ready = sem("out_ready")
    out_stored = [sem("out_stored0"), sem("out_stored1")]
    rows_down = sem("rows_down")
    dve_step = sem("dve_step")

    w_in_v = w_in[0].rearrange("(c p) n -> p c n", p=P)
    gate_v = w_ffn_gate[0].rearrange("(c p) n -> p c n", p=P)
    up_v = w_ffn_up[0].rearrange("(c p) n -> p c n", p=P)
    x_v = x[0].rearrange("(t p) d -> p t d", p=P)
    out_v = out[0].rearrange("(t p) d -> p t d", p=P)

    def f32(ap):
        return ap.bitcast(F32)

    def unit(u):
        return u % SLOTS

    def own(h):
        return slice(h * DH, (h + 1) * DH)

    def other(h):
        return own(1 - h)

    def score_no(p, i, h):
        return (p * ST + i) * 2 + h + 1

    def by_key(buf, h, i):
        row = buf[:, h, i * P:(i + 1) * P]
        return bass.AP(row.tensor, row.offset, [row.ap[0], [PT_STRIDE, i + 1], [1, P]])

    def blocks(bank, n):
        return psum[:, bank, 0:n * P].rearrange("p (j c) -> p j c", c=P)

    def rstd_bank(n):
        return B_OUT if n < YT - 2 else B_TRANS + 1

    def mean_squares(n):
        return psum[:, B_OUT + 1 if n < YT - 2 else B_TRANS, 0:2 * ST]

    def x1_blocks(s, b):
        return psum[:, 2 * s + b, :].rearrange("p (c n) -> p c n", n=P)

    def heads(part):
        return vv[:, :, :, part * DH:(part + 1) * DH]

    def v_blocks():
        return psum[:, B_TRANS, :].rearrange("p (t h c) -> p t h c", t=ST, h=2)

    def wait_y(eng, n):
        if n < LT:
            eng.wait_ge(lru_done, n + 1)
        else:
            eng.wait_ge(half_added, 2 * (n - LT) + 2)

    R_CONV, R_CONVB, R_BR = 0, CW * LT, (CW + 1) * LT
    R_BI, R_LAM, R_G = R_BR + LT, R_BR + 2 * LT, R_BR + 3 * LT
    NPAR = R_G + YT
    PAR_DMAS = 7
    DOWN_TURNS = (FT - 6) // 4

    ATANH = [1.0 / (2 * n + 1) for n in range(1, 9)]

    block = ctx.enter_context(nc.Block())

    @block.sync
    def _(sp):
        def load(u, dst, src):
            if u >= SLOTS:
                sp.wait_ge(w_lo_done, u - SLOTS + 1)
            sp.dma_start(dst, src).then_inc(raw_in[unit(u)], 16)

        def by_chunk(u):
            return raw[:, unit(u), :].rearrange("p (c n) -> p c n", c=DC)

        W = D // ST
        for g in range(ST):
            sp.dma_start(x_nat[:, :, g * W:(g + 1) * W], x_v[:, :, g * W:(g + 1) * W]).then_inc(x_in[g], 16)
            if g == 0:
                load(0, by_chunk(0), w_in_v[:, :, proj_col[0]:proj_col[0] + P])
        for u in range(1, U_OUT):
            if u == 2:
                for src, r, n in ((conv_w[0].rearrange("j (t p) -> (j t) p", p=P), R_CONV, CW * LT),
                                  (conv_b[0].rearrange("(t p) -> t p", p=P), R_CONVB, LT),
                                  (b_rgate[0].rearrange("(t p) -> t p", p=P), R_BR, LT),
                                  (b_igate[0].rearrange("(t p) -> t p", p=P), R_BI, LT),
                                  (lru_lambda[0].rearrange("(t p) -> t p", p=P), R_LAM, LT),
                                  (out_norm_g[0].rearrange("(t p) -> t p", p=P), R_G, YT)):
                    sp.dma_start(par_rows[r:r + n, :], src).then_inc(par_in, 16)
                sp.dma_start(bf[:, :], b_fgate[0].rearrange("(h a) -> h a", a=1)).then_inc(par_in, 16)
            load(u, by_chunk(u), w_in_v[:, :, proj_col[u]:proj_col[u] + P])
        sp.wait_ge(fox_ready, 4)
        for i, v in enumerate((ln1_g, ln1_b)):
            sp.dma_start(gb[:, i, :], v[0].partition_broadcast(P)).then_inc(gb_in, 16)
        for n, m in enumerate(y_tile):
            load(U_OUT + n, raw[:, unit(U_OUT + n), :], w_out[0, m * P:(m + 1) * P, :])
        with sp.Fori(0, FT // 2) as it:
            for k in range(4):
                u = U_FFN + k
                sp.wait_ge(w_lo_done, it * 4 + (u - SLOTS + 1))
                sp.dma_start(by_chunk(u), (gate_v, up_v)[k % 2][:, :, bass.ds(it * (2 * P) + (k // 2) * P, P)])\
                  .then_inc(raw_in[unit(u)], 16)
        for i, v in enumerate((ln2_g, ln2_b)):
            sp.wait_ge(x1_done, 2 * ST)
            sp.dma_start(gb[:, i, :], v[0].partition_broadcast(P)).then_inc(gb_in, 16)
        for f in range(FT):
            load(U_DOWN + f, raw[:, unit(U_DOWN + f), :], w_ffn_down[0, f * P:(f + 1) * P, :])
        for s in range(ST):
            for b in range(2 if s < ST - 1 else 1):
                cols = slice(b * BN, (b + 1) * BN)
                sp.wait_ge(out_ready, 2 * s + b + 1)
                sp.dma_start(out_v[:, s, cols], z[:, s % 2, cols]).then_inc(out_stored[s % 2], 16)
        for b in range(2):
            sp.wait_ge(out_stored[b], 32 * (ST // 2))

    @block.gpsimd
    def _(pool):
        steps = [0]

        def settle(ins):
            steps[0] += 1
            ins.then_inc(pool_step, 1)
            pool.wait_ge(pool_step, steps[0])

        settle(nc.gpsimd.memset(ident[:, :], 0.0))
        nc.gpsimd.affine_select(out=ident[:, :], in_=ident[:, :], compare_op=ALU.not_equal, fill=1.0, base=0,
                                pattern=[[-1, P]], channel_multiplier=1).then_inc(ident_made, 1)
        settle(nc.gpsimd.memset(gate_w[:, :, :], 0.0))
        for g, w in enumerate((w_rgate, w_igate)):
            for t in range(LT):
                for b in range(2):
                    pool.dma_start(gate_w[b * DH:(b + 1) * DH, g * LT + t, b * DH:(b + 1) * DH],
                                   w[0, 2 * t + b, :, :]).then_inc(gate_in, 16)
        nc.gpsimd.memset(xb[:, :, 0:CW - 1], 0.0).then_inc(pad_made, 1)
        settle(nc.gpsimd.memset(eps[:, 0:1], RMS_EPS))
        settle(nc.gpsimd.memset(eps[:, 1:2], LN_EPS))
        settle(nc.gpsimd.memset(headmean[:, :], 0.0))
        for b in range(2):
            settle(nc.gpsimd.memset(headmean[b * DH:(b + 1) * DH, b:b + 1], 1.0 / DH))
        settle(nc.gpsimd.memset(mask[:, :], 0.0))
        settle(nc.gpsimd.affine_select(out=mask[:, S - P:S], in_=mask[:, S - P:S], compare_op=ALU.is_ge, fill=BIG,
                                       base=0, pattern=[[-1, P]], channel_multiplier=1))
        settle(nc.gpsimd.memset(onehot[:, :], 0.0))
        for b in range(4):
            settle(nc.gpsimd.affine_select(out=onehot[:, :], in_=onehot[:, :], compare_op=ALU.not_equal, fill=1.0,
                                           base=-32 * b, pattern=[[-1, NFOX]], channel_multiplier=1))
        settle(nc.gpsimd.memset(f32(fox_g[:, :]), 0.0))
        settle(nc.gpsimd.memset(f32(fox_k[:, :]), 0.0))
        for b, (buf, v) in enumerate(((fox_g, 1.0), (fox_g, 1.0), (fox_k, -1.0), (fox_k, -1.0))):
            ins = nc.gpsimd.memset(f32(buf[32 * b:32 * b + NFOX, :]), v)
            if b < 3:
                settle(ins)
        ins.then_inc(consts_made, 1)

        def copy_keys(p):
            for h in range(2):
                pool.wait_ge(k_hi_done, 2 * p + h + 1)
                if p >= 2:
                    pool.wait_ge(scores, score_no(p - 2, ST - 1, 1))
                nc.gpsimd.tensor_copy(kk[other(h), p % 2, h, :], f32(kk[own(h), p % 2, h, :])).then_inc(k_copied, 1)
                pool.wait_ge(k_copied, 2 * p + h + 1)

        def add_times(dst, a, c, b):
            settle(nc.gpsimd.tensor_scalar(fg(0), a, c, None, ALU.add))
            settle(nc.gpsimd.tensor_tensor(dst, fg(0), b, ALU.mult))

        pool.wait_ge(logexp_done, 4)
        pool.wait_ge(ff_read, 1)
        settle(nc.gpsimd.tensor_scalar(fg(3), fg(1), 8.0 / 49, -24.0 / 49, ALU.mult, ALU.add))
        for k in range(3):
            add_times(fg(4), fg(1), 2.0, fg(3))
            add_times(fg(3), fg(4), 2.0, fg(3))
            if k == 0:
                copy_keys(0)
        settle(nc.gpsimd.tensor_tensor(fg(3), fg(1), fg(3), ALU.mult))
        settle(nc.gpsimd.tensor_tensor(fg(4), fg(3), fg(3), ALU.mult))
        settle(nc.gpsimd.tensor_scalar(fg(5), fg(4), ATANH[-1], None, ALU.mult))
        for c in reversed(ATANH[:-1]):
            add_times(fg(5), fg(5), c, fg(4))
            if c == ATANH[6]:
                copy_keys(1)
        add_times(fg(5), fg(5), 1.0, fg(3))
        settle(nc.gpsimd.tensor_scalar(fg(5), fg(5), 2.0, None, ALU.mult))
        nc.gpsimd.tensor_tensor(fg(0), fg(5), fg(2), ALU.add).then_inc(forget_log, 1)
        copy_keys(2)
        pool.wait_ge(forget_sum, 1)
        f_hi = f32(fox_k[0:NFOX, :])
        nc.gpsimd.tensor_copy(fox_k[0:NFOX, :], fg(1)).then_inc(fox_ready, 1)
        nc.gpsimd.tensor_copy(fox_g[64:64 + NFOX, :], fg(1)).then_inc(fox_ready, 1)
        pool.wait_ge(fox_ready, 2)
        nc.gpsimd.tensor_tensor(fox_k[32:32 + NFOX, :], fg(1), f_hi, ALU.subtract).then_inc(fox_ready, 1)
        nc.gpsimd.tensor_tensor(fox_g[96:96 + NFOX, :], fg(1), f_hi, ALU.subtract).then_inc(fox_ready, 1)
        pool.wait_ge(fox_ready, 4)
        for p in range(MOBAP, PAIRS):
            pool.wait_ge(scores, score_no(p - 1, ST - 1, 1))
            for h in range(2):
                head = 2 * (p - MOBAP) + h
                nc.gpsimd.tensor_scalar(fox_q[:, h, :], f32(fox_g[:, :]), onehot[:, head:head + 1], None, ALU.mult)\
                  .then_inc(fox_q_done, 1)
            pool.wait_ge(fox_q_done, 2 * (p - MOBAP) + 2)
            copy_keys(p)

        def split_w(u):
            pool.wait_ge(w_lo_done, u)
            pool.wait_ge(w_hi_done, u + 1)
            nc.gpsimd.tensor_tensor(w_lo[:, unit(u), :], raw[:, unit(u), :], f32(w_hi[:, unit(u), :]), ALU.subtract)\
              .then_inc(w_lo_done, 1)

        for u in range(U_OUT + 2, U_OUT + SLOTS):
            split_w(u)

        def refine_root(n, s):
            k = n * ST + s
            r, t = rstd_ln[:, s % 2:s % 2 + 1], root_t[:, s % 2, :]
            if k >= 2:
                pool.wait_ge(x1_done, min(2 * (k - 1), 2 * ST))
                if k - 2 >= ST:
                    pool.wait_ge(out_ready, 2 * (k - 1 - ST))
            pool.wait_ge(var_done, k + 1)
            settle(nc.gpsimd.tensor_scalar(t[:, 0:1], mv[:, s % 2, 1:2], LN_EPS, None, ALU.add))
            pool.wait_ge(rstd_ln_done, k + 1)
            settle(nc.gpsimd.tensor_tensor(t[:, 1:2], t[:, 0:1], r, ALU.mult))
            settle(nc.gpsimd.tensor_tensor(t[:, 1:2], t[:, 1:2], r, ALU.mult))
            settle(nc.gpsimd.tensor_scalar(t[:, 1:2], t[:, 1:2], -0.5, 1.5, ALU.mult, ALU.add))
            nc.gpsimd.tensor_tensor(t[:, 2:3], t[:, 1:2], r, ALU.mult).then_inc(root_refined, 1)

        for s in range(ST - 1):
            refine_root(0, s)
        for u in range(U_FFN, U_FFN + 2):
            split_w(u)
        refine_root(0, ST - 1)
        for s in range(ST):
            refine_root(1, s)

    @block.scalar
    def _(act):
        def split_w(u, turn=0):
            act.wait_ge(raw_in[unit(u)], turn * 16 + 16 * (u // SLOTS + 1))
            if u >= SLOTS:
                act.wait_ge(unit_used, turn * 4 + (u - SLOTS + 1))
            nc.scalar.activation(w_hi[:, unit(u), :], raw[:, unit(u), :], ACT.Copy).then_inc(w_hi_done, 1)

        for c in range(DC):
            if c == 2:
                split_w(0)
            act.wait_ge(x_tr, c + 1)
            nc.scalar.activation(a_hi[:, c, :], psum[:, 2 + c % 6, :], ACT.Copy).then_inc(x_hi_done, 1)
        split_w(1)
        for t in range(LT):
            split_w(t + 2)
            act.wait_ge(unit_used, t + 1)
            nc.scalar.activation(xb[:, t, CW - 1:], psum[:, t % 2, :], ACT.Copy).then_inc(xb_done, 1)
        for t in range(LT):
            split_w(LT + t + 2)
            act.wait_ge(unit_used, LT + t + 1)
            nc.scalar.activation(lg[:, t, :], psum[:, (LT + t) % 2, :], ACT.Gelu_apprx_tanh).then_inc(gelu_done, 1)
        act.wait_ge(gates_mm, 1)
        act.wait_ge(par_done, 1)
        for g in range(2):
            for t in range(LT):
                b = (R_BR, R_BI)[g] + t
                nc.scalar.activation(ri[:, g, t, :], psum[:, 2 + g * LT + t, :], ACT.Sigmoid,
                                     bias=par[:, b:b + 1]).then_inc(gates_done, 1)
        split_w(U_FF + 2)
        nc.scalar.activation(lam[:, 0, :], par[:, R_LAM:R_LAM + LT], ACT.Abs).then_inc(logexp_done, 1)
        act.wait_ge(logexp_done, 1)
        nc.scalar.activation(lam[:, 1, :], lam[:, 0, :], ACT.Exp, scale=-1.0).then_inc(logexp_done, 1)
        act.wait_ge(unit_used, U_FF + 1)
        act.wait_ge(par_in, 16 * PAR_DMAS)
        nc.scalar.activation(fg(0), psum[0:NFOX, U_FF % 2, :], ACT.Abs, bias=bf[:, 0:1]).then_inc(logexp_done, 1)
        act.wait_ge(logexp_done, 3)
        nc.scalar.activation(fg(1), fg(0), ACT.Exp, scale=-1.0).then_inc(logexp_done, 1)
        split_w(U_QKV + 2)
        act.wait_ge(log_decay_done, 2)
        act.wait_ge(gates_done, LT)
        for t in range(LT):
            nc.scalar.activation(a_t[:, t, :], ri[:, 0, t, :], ACT.Exp, scale=lam[:, 6, t:t + 1]).then_inc(decay_done, 1)
            nc.scalar.activation(th[:, t, :], ri[:, 0, t, :], ACT.Tanh, scale=lam[:, 7, t:t + 1]).then_inc(decay_done, 1)


        def q_high(p, u):
            act.wait_ge(unit_used, u + 1)
            for h in range(2):
                nc.scalar.activation(qq[own(h), p % 2, h, :], psum[own(h), u % 2, :], ACT.Copy, scale=-SCALE)\
                  .then_inc(q_hi_done, 1)

        def k_high(p, u):
            act.wait_ge(unit_used, u + 1)
            for h in range(2):
                nc.scalar.activation(kk[own(h), p % 2, h, :], psum[own(h), u % 2, :], ACT.Copy).then_inc(k_hi_done, 1)

        def v_copy(p, u):
            act.wait_ge(unit_used, u + 1)
            if p >= 1:
                act.wait_ge(v_tr, p)
            nc.scalar.activation(vT[:, :], psum[:, u % 2, :], ACT.Copy).then_inc(vT_done, 1)

        def square(n):
            wait_y(act, n)
            if n >= 1:
                act.wait_ge(ms_mm, n)
            nc.scalar.activation(sq[:, :], yraw[:, n % 2, :], ACT.Square).then_inc(sq_done, 1)

        def rms(n):
            act.wait_ge(ms_mm, n + 1)
            if n >= 1:
                act.wait_ge(rstd_spread, n)
            nc.scalar.activation(log_ms[:, :], mean_squares(n), ACT.Ln, bias=eps[:, 0:1]).then_inc(ms_read, 1)
            act.wait_ge(ms_read, n + 1)
            nc.scalar.activation(rstd[:, :, :], log_ms[:, :].unsqueeze(2).to_broadcast([P, ST * 2, DH]), ACT.Exp,
                                 scale=-0.5).then_inc(rstd_done, 1)

        def rstd_rows(n, s):
            k = n * ST + s
            act.wait_ge(var_done, k + 1)
            r = rstd_ln[:, s % 2:s % 2 + 1]
            nc.scalar.activation(r, mv[:, s % 2, 1:2], ACT.Ln, bias=eps[:, 1:2]).then_inc(var_log, 1)
            act.wait_ge(var_log, k + 1)
            nc.scalar.activation(r, r, ACT.Exp, scale=-0.5).then_inc(rstd_ln_done, 1)

        def y_high(n):
            act.wait_ge(yn_done, n + 1)
            act.wait_ge(unit_used, U_OUT)
            nc.scalar.activation(a_hi[:, n, :], yn[:, n, :], ACT.Copy).then_inc(y_hi_done, 1)

        def exponentials(p, i):
            for h in range(2):
                n = score_no(p, i, h)
                act.wait_ge(masked, n)
                if n > 4:
                    act.wait_ge(p_tr, n - 4)
                nc.scalar.activation(prob[:, i % 2, h, 0:(i + 1) * P], smask[:, h, 0:(i + 1) * P], ACT.Exp, scale=-1.0,
                                     bias=nmax[:, h:h + 1], accum_out=rsum[:, h:h + 1]).then_inc(exps, 1)

        def transposed_hi(p, i):
            for h in range(2):
                act.wait_ge(p_tr, score_no(p, i, h))
                if i == 0 and p >= 1:
                    act.wait_ge(pv_done, 2 * (p - 1) + h + 1)
                nc.scalar.activation(by_key(pt_hi, h, i), blocks(B_TRANS + h, i + 1), ACT.Copy).then_inc(pt_hi_done, 1)

        def attend(p, u):
            more = p + 1 < PAIRS
            if not more:
                y_high(0)
            act.wait_ge(v_tr, p + 1)
            if p >= 1:
                act.wait_ge(pv_done, 2 * p)
            nc.scalar.activation(heads(0), v_blocks(), ACT.Copy).then_inc(v_hi_done, 1)
            exponentials(p, 0)
            if more:
                if p >= 1:
                    values_out(p - 1)
            else:
                y_high(1)
            split_w(u + 2)
            exponentials(p, 1)
            if p == 0:
                act.wait_ge(lru_done, LT)
            transposed_hi(p, 0)
            if more:
                square(p + 1 if p else 0)
                q_high(p + 1, u)
            else:
                values_out(p - 1)
                split_w(u + 3)
                y_high(2)
            exponentials(p, 2)
            if p == 0:
                act.wait_ge(consts_made, 1)
                rms(0)
            transposed_hi(p, 1)
            if p == 0:
                square(1)
            elif more:
                rms(p + 1)
            else:
                y_high(3)
            if more:
                split_w(u + 3)
            exponentials(p, 3)
            transposed_hi(p, 2)
            if p == 0:
                rms(1)
            if more:
                k_high(p + 1, u + 1)
            transposed_hi(p, 3)
            if more:
                split_w(u + 4)
                v_copy(p + 1, u + 2)

        def values_out(p):
            for h in range(2):
                act.wait_ge(pv_done, 2 * p + h + 1)
                if p >= 1:
                    act.wait_ge(half_added, 2 * p + h - 1)
                nc.scalar.activation(otmp[:, h, :], psum[DH:P, B_OUT + h, :], ACT.Copy).then_inc(o_copied, 1)

        q_high(0, U_QKV)
        k_high(0, U_QKV + 1)
        act.wait_ge(root_arg, 1)
        nc.scalar.activation(th[:, :, :], th[:, :, :], ACT.Sqrt).then_inc(root_done, 1)
        split_w(U_QKV + 3)
        split_w(U_QKV + 4)
        nc.scalar.preload_act_table_set("natural_log_exp_and_others")
        v_copy(0, U_QKV + 2)
        for p in range(PAIRS):
            attend(p, U_QKV + 3 * (p + 1))
        square(YT - 2)
        values_out(PAIRS - 1)
        rms(YT - 2)
        y_high(YT - 4)
        square(YT - 1)
        y_high(YT - 3)
        rms(YT - 1)
        for n in range(YT - 2, YT):
            y_high(n)
        for n in range(SLOTS, YT):
            split_w(U_OUT + n)

        def x1_high(s):
            for b in range(2):
                act.wait_ge(x1_tr, 2 * s + b + 1)
                nc.scalar.activation(a_hi[:, 4 * b:4 * b + 4, s * P:(s + 1) * P], x1_blocks(s, b), ACT.Copy)\
                  .then_inc(x1_hi_done, 1)

        rstd_rows(0, 0)
        for s in range(1, ST - 1):
            rstd_rows(0, s)
            if s == ST - 2:
                split_w(U_FFN)
            x1_high(s - 1)
        split_w(U_FFN + 1)
        x1_high(ST - 2)
        rstd_rows(0, ST - 1)
        x1_high(ST - 1)

        def ffn_turn(it):
            for f in range(2):
                for k in range(2):
                    split_w(U_FFN + 2 + 2 * f + k, it)
                act.wait_ge(unit_used, it * 4 + (U_FFN + 2 * f + 1))
                if it is not first:
                    act.wait_ge(hid_done, it * 2 + (f - 1))
                nc.scalar.activation(silu[:, f, :], psum[:, 2 * f, :], ACT.Silu).then_inc(silu_done, 1)

        first = 0
        ffn_turn(first)
        with act.Fori(1, FT // 2 - 1) as it:
            ffn_turn(it)

        def split_h(f, turn=0):
            if f >= SLOTS:
                act.wait_ge(unit_used, turn * 4 + (U_DOWN + f - SLOTS + 1))
            act.wait_ge(hid_done, turn * 4 + (f + 1))
            nc.scalar.activation(h_hi[:, f % SLOTS, :], hid[:, bass.ds(turn * (4 * S) + f * S, S)], ACT.Copy)\
              .then_inc(h_hi_done, 1)

        split_h(0)
        split_h(1)
        ffn_turn(FT // 2 - 1)
        for f in range(2, 4):
            split_w(U_DOWN + f)
            split_h(f)
        with act.Fori(0, DOWN_TURNS) as it:
            for f in range(4, 8):
                split_w(U_DOWN + f, it)
                split_h(f, it)
        for f in range(FT - 2, FT):
            split_w(U_DOWN + f)
            split_h(f)
        nc.scalar.preload_act_table_set("natural_log_exp_and_others")
        for s in range(ST):
            rstd_rows(1, s)
        act.wait_ge(out_ready, 2 * ST)
        act.dma_start(out_v[:, ST - 1, BN:], z[:, (ST - 1) % 2, BN:]).then_inc(out_stored[(ST - 1) % 2], 16)

    @block.vector
    def _(dve):
        steps = [0]

        def step(ins):
            steps[0] += 1
            ins.then_inc(dve_step, 1)
            return steps[0]

        def settled(n=None):
            dve.wait_ge(dve_step, n or steps[0])

        def split_w(u, turn=0):
            dve.wait_ge(w_hi_done, turn * 4 + (u + 1))
            nc.vector.tensor_tensor(w_lo[:, unit(u), :], raw[:, unit(u), :], f32(w_hi[:, unit(u), :]), ALU.subtract)\
              .then_inc(w_lo_done, 1)

        def log_sigmoid(t):
            step(nc.vector.tensor_scalar(t(3), t(1), 2.0, None, ALU.add))
            settled()
            step(nc.vector.reciprocal(t(4), t(3)))
            settled()
            step(nc.vector.tensor_tensor(t(3), t(1), t(4), ALU.mult))
            settled()
            step(nc.vector.tensor_tensor(t(4), t(3), t(3), ALU.mult))
            settled()
            step(nc.vector.tensor_scalar(t(5), t(4), ATANH[-1], None, ALU.mult))
            for c in reversed(ATANH[:-1]):
                settled()
                step(nc.vector.scalar_tensor_tensor(t(5), t(5), c, t(4), ALU.add, ALU.mult))
            settled()
            step(nc.vector.scalar_tensor_tensor(t(5), t(5), 1.0, t(3), ALU.add, ALU.mult))
            settled()
            step(nc.vector.scalar_tensor_tensor(t(0), t(5), -2.0, t(2), ALU.mult, ALU.add))
            settled()

        def q_low(p, u):
            dve.wait_ge(q_hi_done, 2 * p + 2)
            for h in range(2):
                nc.vector.scalar_tensor_tensor(qq[other(h), p % 2, h, :], psum[own(h), u % 2, :], -SCALE,
                                               f32(qq[own(h), p % 2, h, :]), ALU.mult, ALU.subtract)\
                  .then_inc(q_lo_done, 1)

        def k_low(p, u):
            dve.wait_ge(k_hi_done, 2 * p + 2)
            for h in range(2):
                nc.vector.tensor_tensor(k_lo[own(h), p % 2, :], psum[own(h), u % 2, :], f32(kk[own(h), p % 2, h, :]),
                                        ALU.subtract).then_inc(k_lo_done, 1)

        for c in range(DC):
            if c == 2:
                split_w(0)
            dve.wait_ge(x_hi_done, c + 1)
            nc.vector.tensor_tensor(a_lo[:, c, :], psum[:, 2 + c % 6, :], f32(a_hi[:, c, :]), ALU.subtract)\
              .then_inc(x_lo_done, 1)
        split_w(1)
        dve.wait_ge(par_tr, 1)
        nc.vector.tensor_copy(par[:, 0:NPAR], psum[:, 7, 0:NPAR]).then_inc(par_done, 1)
        dve.wait_ge(par_done, 1)
        for t in range(LT):
            split_w(t + 2)
            dve.wait_ge(xb_done, t + 1)
            dve.wait_ge(pad_made, 1)

            def tap(j):
                n = R_CONV + j * LT + t
                return xb[:, t, j:j + S], par[:, n:n + 1]

            src, w = tap(CW - 1)
            step(nc.vector.tensor_scalar(xc[:, t, :], src, w, par[:, R_CONVB + t:R_CONVB + t + 1], ALU.mult, ALU.add))
            for j in reversed(range(CW - 1)):
                src, w = tap(j)
                settled()
                ins = nc.vector.scalar_tensor_tensor(xc[:, t, :], src, w, xc[:, t, :], ALU.mult, ALU.add)
                if j:
                    step(ins)
            ins.then_inc(conv_done, 1)
        split_w(LT + 2)
        split_w(LT + 3)
        split_w(LT + 4)
        dve.wait_ge(logexp_done, 2)
        step(nc.vector.tensor_scalar(lam[:, 2, :], par[:, R_LAM:R_LAM + LT], 0.0, None, ALU.min))
        log_sigmoid(lambda k: lam[:, k, :])
        for k, sign in ((6, 1.0), (7, -1.0)):
            nc.vector.tensor_scalar(lam[:, k, :], lam[:, 0, :], sign * LRU_C, None, ALU.mult).then_inc(log_decay_done, 1)
        dve.wait_ge(logexp_done, 4)
        nc.vector.tensor_scalar(fg(2), psum[0:NFOX, U_FF % 2, :], bf[:, 0:1], 0.0, ALU.add, ALU.min)\
          .then_inc(ff_read, 1)
        split_w(U_QKV + 2)
        q_low(0, U_QKV)
        dve.wait_ge(decay_done, 2 * LT)
        dve.wait_ge(gates_done, 2 * LT)
        sq_a = xb[:, :, 0:S]
        step(nc.vector.tensor_tensor(sq_a, a_t[:, :, :], a_t[:, :, :], ALU.mult))
        settled()
        step(nc.vector.scalar_tensor_tensor(th[:, :, :], sq_a, 1.0, th[:, :, :], ALU.add, ALU.mult))
        settled()
        nc.vector.tensor_scalar(th[:, :, :], th[:, :, :], 1e-32, None, ALU.max).then_inc(root_arg, 1)
        k_low(0, U_QKV + 1)
        split_w(U_QKV + 3)
        step(nc.vector.tensor_tensor(xc[:, :, :], ri[:, 1, :, :], xc[:, :, :], ALU.mult))
        split_w(U_QKV + 4)
        dve.wait_ge(root_done, 1)
        settled()
        step(nc.vector.tensor_tensor(th[:, :, :], th[:, :, :], xc[:, :, :], ALU.mult))

        def recurrence():
            settled()
            for t in range(LT):
                step(nc.vector.tensor_tensor_scan(xb[:, t, 0:S], a_t[:, t, :], th[:, t, :], 0.0, ALU.mult, ALU.add))
            dve.wait_ge(gelu_done, LT)
            settled()
            for t in range(LT):
                nc.vector.tensor_tensor(yraw[:, t, :], xb[:, t, 0:S], lg[:, t, :], ALU.mult).then_inc(lru_done, 1)

        def norm(n):
            dve.wait_ge(rstd_spread, n + 1)
            g = R_G + y_tile[n]
            nc.vector.scalar_tensor_tensor(yn[:, n, :], yraw[:, n % 2, :], par[:, g:g + 1],
                                           psum[:, rstd_bank(n), :], ALU.mult, ALU.mult).then_inc(yn_done, 1)

        def y_low(n):
            dve.wait_ge(y_hi_done, n + 1)
            nc.vector.tensor_tensor(a_lo[:, n, :], yn[:, n, :], f32(a_hi[:, n, :]), ALU.subtract).then_inc(y_lo_done, 1)

        def mask_scores(p, i):
            w = (i + 1) * P
            for h in range(2):
                n = score_no(p, i, h)
                dve.wait_ge(scores, n)
                if n > 2:
                    dve.wait_ge(exps, n - 2)
                nc.vector.tensor_tensor_reduce(out=smask[:, h, 0:w], in0=psum[:, B_SCORE + h, 0:w], in1=mask[:, S - w:S],
                                               scale=1.0, scalar=BIG, op0=ALU.add, op1=ALU.min,
                                               accum_out=nmax[:, h:h + 1]).then_inc(masked, 1)

        def normalise(p, i):
            for h in range(2):
                dve.wait_ge(exps, score_no(p, i, h))
                step(nc.vector.reciprocal(rinv[:, h:h + 1], rsum[:, h:h + 1]))
            for h in range(2):
                settled()
                row = prob[:, i % 2, h, 0:(i + 1) * P]
                nc.vector.tensor_scalar(row, row, rinv[:, h:h + 1], None, ALU.mult).then_inc(probs, 1)

        def transposed_lo(p, i):
            for h in range(2):
                dve.wait_ge(pt_hi_done, score_no(p, i, h))
                nc.vector.tensor_tensor(by_key(pt_lo, h, i), blocks(B_TRANS + h, i + 1), f32(by_key(pt_hi, h, i)),
                                        ALU.subtract).then_inc(pt_lo_done, 1)

        def attend(p, u):
            more = p + 1 < PAIRS
            if not more:
                y_low(0)
            mask_scores(p, 0)
            dve.wait_ge(v_hi_done, p + 1)
            nc.vector.tensor_tensor(heads(1), v_blocks(), f32(heads(0)), ALU.subtract).then_inc(v_lo_done, 1)
            normalise(p, 0)
            if not more:
                y_low(1)
            mask_scores(p, 1)
            if p == 0:
                recurrence()
            if more:
                if p >= 1:
                    values_sum(p - 1)
                split_w(u + 2)
            normalise(p, 1)
            transposed_lo(p, 0)
            if p == MOBAP - 1:
                dve.wait_ge(forget_log, 1)
                nc.vector.tensor_tensor_scan(fg(1), f32(fox_g[0:NFOX, :]), fg(0), 0.0, ALU.mult, ALU.add)\
                  .then_inc(forget_sum, 1)
            mask_scores(p, 2)
            if more:
                q_low(p + 1, u)
            else:
                y_low(2)
            transposed_lo(p, 1)
            normalise(p, 2)
            if p == 0:
                norm(0)
            mask_scores(p, 3)
            if more:
                split_w(u + 3)
            else:
                y_low(3)
            normalise(p, 3)
            transposed_lo(p, 2)
            if more:
                norm(p + 1)
                k_low(p + 1, u + 1)
            else:
                values_sum(p - 1)
            transposed_lo(p, 3)
            if more:
                split_w(u + 4)

        def values_sum(p):
            for h in range(2):
                dve.wait_ge(o_copied, 2 * p + h + 1)
                nc.vector.tensor_tensor(yraw[h * DH:(h + 1) * DH, (p + LT) % 2, :], psum[0:DH, B_OUT + h, :],
                                        otmp[:, h, :], ALU.add).then_inc(half_added, 1)

        dve.wait_ge(consts_made, 1)
        for p in range(PAIRS):
            attend(p, U_QKV + 3 * (p + 1))
        values_sum(PAIRS - 1)
        norm(YT - 2)
        for n in range(YT - 4, YT - 2):
            y_low(n)
        norm(YT - 1)
        for n in range(YT - 2, YT):
            y_low(n)
        dve.wait_ge(w_lo_done, U_OUT + SLOTS)
        for n in range(SLOTS, YT):
            split_w(U_OUT + n)

        def layer_norm(n, s, dst, summed, done):
            k = n * ST + s
            m = mv[:, s % 2, :]
            root = root_t[:, s % 2, 2:3]
            half = [slice(b * BN, (b + 1) * BN) for b in range(2)]
            zs = [z[:, s % 2, half[b]] for b in range(2)]
            added = []
            for b in range(2):
                dve.wait_ge(summed, 2 * s + b + 1)
                added.append(step(nc.vector.scalar_tensor_tensor(zs[b], x_nat[:, s, half[b]], ALPHA,
                                                                 psum[:, 2 * s + b, :], ALU.mult, ALU.add)))
            for b in range(2):
                settled(added[b])
                step(nc.vector.bn_stats(stats[:, s % 2, b, :], zs[b]))
            settled()
            nc.vector.bn_aggr(m, stats[:, s % 2, :, :].rearrange("p b k -> p (b k)")).then_inc(var_done, 1)
            dve.wait_ge(var_done, k + 1)
            scaled = [step(nc.vector.scalar_tensor_tensor(zs[b], zs[b], m[:, 0:1], gb[:, 0, half[b]],
                                                          ALU.subtract, ALU.mult)) for b in range(2)]
            dve.wait_ge(root_refined, k + 1)
            for b in range(2):
                settled(scaled[b])
                nc.vector.scalar_tensor_tensor(dst[:, half[b]], zs[b], root, gb[:, 1, half[b]],
                                               ALU.mult, ALU.add).then_inc(done, 1)

        def x1_low(s):
            for b in range(2):
                dve.wait_ge(x1_hi_done, 2 * s + b + 1)
                cols = slice(s * P, (s + 1) * P)
                nc.vector.tensor_tensor(a_lo[:, 4 * b:4 * b + 4, cols], x1_blocks(s, b),
                                        f32(a_hi[:, 4 * b:4 * b + 4, cols]), ALU.subtract).then_inc(x1_lo_done, 1)

        dve.wait_ge(gb_in, 32)
        for s in range(ST):
            layer_norm(0, s, x_nat[:, s, :], rows_mixed, x1_done)
            if s >= 1:
                x1_low(s - 1)
        x1_low(ST - 1)
        dve.wait_ge(w_lo_done, U_FFN + 2)

        def ffn_turn(it):
            for f in range(2):
                for k in range(2):
                    split_w(U_FFN + 2 + 2 * f + k, it)
                dve.wait_ge(silu_done, it * 2 + (f + 1))
                dve.wait_ge(unit_used, it * 4 + (U_FFN + 2 * f + 2))
                nc.vector.tensor_tensor(hid[:, bass.ds(it * (2 * S) + f * S, S)], psum[:, 2 * f + 1, :], silu[:, f, :],
                                        ALU.mult).then_inc(hid_done, 1)

        ffn_turn(0)
        with dve.Fori(1, FT // 2 - 1) as it:
            ffn_turn(it)

        def split_h(f, turn=0):
            dve.wait_ge(h_hi_done, turn * 4 + (f + 1))
            nc.vector.tensor_tensor(h_lo[:, f % SLOTS, :], hid[:, bass.ds(turn * (4 * S) + f * S, S)],
                                    f32(h_hi[:, f % SLOTS, :]), ALU.subtract).then_inc(h_lo_done, 1)

        split_h(0)
        split_h(1)
        ffn_turn(FT // 2 - 1)
        for f in range(2, 4):
            split_w(U_DOWN + f)
            split_h(f)
        with dve.Fori(0, DOWN_TURNS) as it:
            for f in range(4, 8):
                split_w(U_DOWN + f, it)
                split_h(f, it)
        for f in range(FT - 2, FT):
            split_w(U_DOWN + f)
            split_h(f)
        dve.wait_ge(gb_in, 64)
        for s in range(ST):
            if s >= 2:
                dve.wait_ge(out_stored[s % 2], 32 * (s // 2))
            layer_norm(1, s, z[:, s % 2, :], rows_down, out_ready)

    @block.tensor
    def _(pe):
        def three(dst, s_hi, s_lo, m_hi, m_lo, start, stop):
            nc.tensor.matmul(dst, s_hi, m_hi, start=start, stop=False)
            nc.tensor.matmul(dst, s_hi, m_lo, start=False, stop=False)
            return nc.tensor.matmul(dst, s_lo, m_hi, start=False, stop=stop)

        def unit_ready(u, turn=0):
            pe.wait_ge(w_lo_done, turn * 4 + (u + 1))

        def chunk(dst, u, c, rows=slice(0, S)):
            cols = slice(c * P, (c + 1) * P)
            return three(dst, w_hi[:, unit(u), cols], w_lo[:, unit(u), cols], a_hi[:, c, rows], a_lo[:, c, rows],
                         c == 0, c == DC - 1)

        def bank_free(u):
            v = u - 2
            if 0 <= v < LT:
                pe.wait_ge(xb_done, v + 1)
            elif LT <= v < 2 * LT:
                pe.wait_ge(gelu_done, v - LT + 1)
            elif v == U_FF:
                pe.wait_ge(ff_read, 1)
            elif v > U_FF:
                p, k = divmod(v - U_QKV, 3)
                pe.wait_ge((q_lo_done, k_lo_done, vT_done)[k], (2 * p + 2, 2 * p + 2, p + 1)[k])

        def project(u, quarter):
            if quarter == 0:
                unit_ready(u)
                bank_free(u)
            for c in range(2 * quarter, 2 * quarter + 2):
                last = chunk(psum[:, u % 2, :], u, c)
            if quarter == 3:
                last.then_inc(unit_used, 1)

        def gates():
            pe.wait_ge(conv_done, LT)
            pe.wait_ge(gate_in, 16 * 4 * LT)
            for g in range(2):
                for t in range(LT):
                    last = nc.tensor.matmul(psum[:, 2 + g * LT + t, :], gate_w[:, g * LT + t, :], xc[:, t, :],
                                            start=True, stop=True)
            last.then_inc(gates_mm, 1)

        def mean_square(n):
            pe.wait_ge(sq_done, n + 1)
            if n >= 1:
                pe.wait_ge(ms_read, n)
            for t in range(ST):
                last = nc.tensor.matmul(mean_squares(n)[:, 2 * t:2 * t + 2], sq[:, t * P:(t + 1) * P], headmean[:, :],
                                        start=True, stop=True)
            last.then_inc(ms_mm, 1)

        def spread_rstd(n):
            pe.wait_ge(rstd_done, n + 1)
            if n >= 1:
                pe.wait_ge(yn_done, n)
            for t in range(ST):
                last = nc.tensor.transpose(psum[:, rstd_bank(n), t * P:(t + 1) * P], rstd[:, 2 * t:2 * t + 2, :]
                                           .rearrange("p h c -> p (h c)"), ident[:, :])
            last.then_inc(rstd_spread, 1)

        def transpose_v(p):
            pe.wait_ge(vT_done, p + 1)
            if p >= 1:
                pe.wait_ge(pt_lo_done, score_no(p - 1, ST - 1, 0))
            for t in range(ST):
                last = nc.tensor.transpose(psum[:, B_TRANS, t * P:(t + 1) * P], vT[:, t * P:(t + 1) * P], ident[:, :])
            last.then_inc(v_tr, 1)

        def score(p, i):
            w = (i + 1) * P
            if i == 0:
                pe.wait_ge(q_lo_done, 2 * p + 2)
                pe.wait_ge(k_lo_done, 2 * p + 2)
                pe.wait_ge(k_copied, 2 * p + 2)
            for h in range(2):
                n = score_no(p, i, h)
                if n > 2:
                    pe.wait_ge(masked, n - 2)
                dst = psum[:, B_SCORE + h, 0:w]
                cols = slice(i * P, (i + 1) * P)
                fox = p >= MOBAP
                if fox:
                    pe.wait_ge(fox_q_done, 2 * (p - MOBAP) + h + 1)
                    nc.tensor.matmul(dst, fox_q[:, h, cols], fox_k[:, 0:w], start=True, stop=False)
                b = p % 2
                nc.tensor.matmul(dst, qq[:, b, h, cols], kk[:, b, h, 0:w], start=not fox, stop=False)
                nc.tensor.matmul(dst, qq[own(h), b, h, cols], k_lo[own(h), b, 0:w], start=False, stop=True)\
                  .then_inc(scores, 1)

        def transpose_p(p, i):
            for h in range(2):
                n = score_no(p, i, h)
                pe.wait_ge(probs, n)
                if n > 2:
                    pe.wait_ge(pt_lo_done, n - 2)
                if i == 0 and h == 0:
                    pe.wait_ge(v_lo_done, p + 1)
                for j in range(i + 1):
                    last = nc.tensor.transpose(psum[:, B_TRANS + h, j * P:(j + 1) * P],
                                               prob[:, i % 2, h, j * P:(j + 1) * P], ident[:, :])
                last.then_inc(p_tr, 1)

        def values(p, h):
            pe.wait_ge(pt_lo_done, score_no(p, ST - 1, h))
            pe.wait_ge(yn_done, min(p + 2, YT - 2))
            if p >= 1:
                pe.wait_ge(half_added, 2 * (p - 1) + h + 1)
            for j in range(ST):
                cols = slice(j * PT_STRIDE + j * P, j * PT_STRIDE + S)
                for buf in (pt_hi, pt_lo):
                    last = nc.tensor.matmul(psum[:, B_OUT + h, j * P:S], vv[:, j, h, :], buf[:, h, cols],
                                            start=(j == 0 and buf is pt_hi), stop=(j == ST - 1 and buf is pt_lo))
            last.then_inc(pv_done, 1)

        def rows_times(s, a_parts, w_slot, first, last_one, only=None):
            hi, lo = (a[:, s * P:(s + 1) * P] for a in a_parts)
            steps = [(hi, w_hi, 0), (hi, w_hi, 1), (hi, w_lo, 0), (hi, w_lo, 1), (lo, w_hi, 0), (lo, w_hi, 1)]
            for k in (only if only is not None else range(6)):
                a, w, half = steps[k]
                last = nc.tensor.matmul(psum[:, 2 * s + half, :], a, w[:, w_slot, half * S:(half + 1) * S],
                                        start=first and k < 2, stop=last_one and k >= 4)
            return last

        HALF = [(0, 2, 4), (1, 3, 5)]

        def mix_rows(s, n, only=None):
            if s == 0 or n >= SLOTS:
                unit_ready(U_OUT + n)
                pe.wait_ge(y_lo_done, n + 1)
            return rows_times(s, (a_hi[:, n, :], a_lo[:, n, :]), unit(U_OUT + n), n == 0, n == YT - 1, only)

        def attend(p, beside):
            take = iter(beside)

            def piece(n=1):
                for _ in range(n):
                    next(take)()

            if p + 1 == PAIRS:
                transpose_v(p)
                score(p, 0)
                piece()
                score(p, 1)
                piece(2)
                transpose_p(p, 0)
                piece()
                score(p, 2)
                piece()
                transpose_p(p, 1)
                piece()
                score(p, 3)
                piece(2)
                transpose_p(p, 2)
                piece(3)
                transpose_p(p, 3)
                piece()
                values(p, 0)
                values(p, 1)
                return
            piece()
            transpose_v(p)
            score(p, 0)
            piece()
            score(p, 1)
            piece()
            transpose_p(p, 0)
            piece()
            score(p, 2)
            piece()
            if p == 0:
                mean_square(0)
                transpose_p(p, 1)
                piece()
            else:
                transpose_p(p, 1)
                mean_square(p + 1)
                piece()
            score(p, 3)
            if p == 0:
                spread_rstd(0)
            transpose_p(p, 2)
            if p == 0:
                piece()
                mean_square(1)
                piece(2)
                spread_rstd(1)
            else:
                spread_rstd(p + 1)
                piece(3)
            transpose_p(p, 3)
            piece()
            values(p, 0)
            piece()
            values(p, 1)
            piece()

        def first_unit(c):
            unit_ready(0)
            pe.wait_ge(x_lo_done, c + 1)
            return chunk(psum[:, 0, :], 0, c)

        pe.wait_ge(ident_made, 1)
        for c in range(DC):
            pe.wait_ge(x_in[c * ST // DC], 16)
            if c >= 6:
                pe.wait_ge(x_lo_done, c - 5)
            for t in range(ST):
                last = nc.tensor.transpose(psum[:, 2 + c % 6, t * P:(t + 1) * P], x_nat[:, t, c * P:(c + 1) * P],
                                           ident[:, :])
            last.then_inc(x_tr, 1)
            if c >= 6:
                first_unit(c - 6)
        for c in range(DC - 6, DC):
            last = first_unit(c)
        last.then_inc(unit_used, 1)
        pe.wait_ge(par_in, 16 * PAR_DMAS)
        nc.tensor.transpose(psum[:, 7, 0:NPAR], par_rows[0:NPAR, :], ident[0:NPAR, 0:NPAR]).then_inc(par_tr, 1)
        for u in range(1, U_FF):
            for quarter in range(4):
                project(u, quarter)
            if u == U_FF - 2:
                gates()
        for u in range(U_FF, U_QKV + 3):
            for quarter in range(4):
                project(u, quarter)
        pe.wait_ge(gates_done, 2 * LT)
        for p in range(PAIRS):
            u = U_QKV + 3 * (p + 1)
            if p + 1 < PAIRS:
                beside = [(lambda v=u + k // 4, q=k % 4: project(v, q)) for k in range(12)]
            else:
                beside = [(lambda n=k // 3, t=k % 3: mix_rows(0, n, (2 * t, 2 * t + 1))) for k in range(12)]
            attend(p, beside)
        pe.wait_ge(masked, score_no(PAIRS - 1, ST - 1, 1))
        mean_square(YT - 2)
        for n in range(SLOTS):
            mix_rows(1, n)
            if n == 2:
                spread_rstd(YT - 2)
        mean_square(YT - 1)
        pe.wait_ge(half_added, 2 * PAIRS)
        for n in range(SLOTS):
            mix_rows(3, n)
            if n == 2:
                spread_rstd(YT - 1)
        pe.wait_ge(yn_done, YT)
        for n in range(SLOTS):
            mix_rows(2, n).then_inc(unit_used, 1)

        def transpose_x1(s):
            for c in range(DC):
                if c % 4 == 0:
                    pe.wait_ge(x1_done, 2 * s + c // 4 + 1)
                last = nc.tensor.transpose(psum[:, 2 * s + c // 4, (c % 4) * P:(c % 4 + 1) * P],
                                           x_nat[:, s, c * P:(c + 1) * P], ident[:, :])
                if c % 4 == 3:
                    last.then_inc(x1_tr, 1)
                elif c == 0 and s == ST - 2:
                    last.then_inc(unit_used, 1)

        for n in range(SLOTS, YT - 1):
            mix_rows(0, n)
        for b in range(2):
            mix_rows(0, YT - 1, HALF[b]).then_inc(rows_mixed, 1)
        for s in range(1, ST):
            for b in range(2):
                for n in range(SLOTS, YT):
                    last = mix_rows(s, n, HALF[b])
                    if s == ST - 1 and b == 1 and n < YT - 1:
                        last.then_inc(unit_used, 1)
                last.then_inc(rows_mixed, 1)
            if s >= 1:
                transpose_x1(s - 1)

        for rows in range(2):
            for k in range(2):
                pe.wait_ge(x1_lo_done, 4 * (rows + 1))
                unit_ready(U_FFN + k)
                for c in range(DC):
                    last = chunk(psum[:, k, rows * (S // 2):(rows + 1) * (S // 2)], U_FFN + k, c,
                                 slice(rows * (S // 2), (rows + 1) * (S // 2)))
                if rows == 1:
                    last.then_inc(unit_used, 1)
            if rows == 0:
                transpose_x1(ST - 1)

        def ffn_turn(it, units=range(4)):
            for k in units:
                unit_ready(U_FFN + k, it)
                if it is not first:
                    pe.wait_ge((silu_done, hid_done)[k % 2], it * 2 + (k // 2 - 1))
                for c in range(DC):
                    last = chunk(psum[:, k, :], U_FFN + k, c)
                last.then_inc(unit_used, 1)

        first = 0
        ffn_turn(first, range(2, 4))
        with pe.Fori(1, FT // 2) as it:
            ffn_turn(it)

        def down(f, s, only=None):
            return rows_times(s, (h_hi[:, f % SLOTS, :], h_lo[:, f % SLOTS, :]), unit(U_DOWN + f),
                              f == 0, f == FT - 1, only)

        def down_ready(f, turn=0):
            unit_ready(U_DOWN + f, turn)
            pe.wait_ge(h_lo_done, turn * 4 + (f + 1))

        for f in range(2):
            down_ready(f)
            for k in range(ST):
                s = (k + 2) % ST
                if f == 0 and s == 0:
                    pe.wait_ge(silu_done, FT)
                    pe.wait_ge(hid_done, FT)
                last = down(f, s)
            last.then_inc(unit_used, 1)
        with pe.Fori(0, DOWN_TURNS) as it:
            for f in range(2, 6):
                down_ready(f, it)
                for s in range(ST):
                    last = down(f, s)
                last.then_inc(unit_used, 1)
        for f in range(FT - 4, FT - 1):
            down_ready(f)
            down(f, 0)
        down_ready(FT - 1)
        for b in range(2):
            down(FT - 1, 0, HALF[b]).then_inc(rows_down, 1)
        for s in range(1, ST):
            for b in range(2):
                for f in range(FT - 4, FT):
                    last = down(f, s, HALF[b])
                last.then_inc(rows_down, 1)

    ctx.close()


_INS = ['x', 'w_in', 'b_fgate', 'conv_w', 'conv_b', 'w_rgate', 'b_rgate', 'w_igate', 'b_igate', 'lru_lambda',
        'out_norm_g', 'w_out', 'ln1_g', 'ln1_b', 'w_ffn_gate', 'w_ffn_up', 'w_ffn_down', 'ln2_g', 'ln2_b']


def kernel(**inputs):
    import numpy as np
    import concourse.bacc as bacc
    from concourse.bass_utils import run_bass_kernel_spmd

    nc = bacc.Bacc("TRN2", target_bir_lowering=False, num_devices=1)
    arrays, args = {}, []
    for name in _INS:
        a = np.ascontiguousarray(inputs[name])
        arrays[f"in_{name}_dram"] = a
        args.append(nc.dram_tensor(f"in_{name}_dram", a.shape, mybir.dt.from_np(a.dtype), kind="ExternalInput").ap())
    shape = np.shape(inputs['x'])
    args.append(nc.dram_tensor("out_0_dram", shape, mybir.dt.float32, kind="ExternalOutput").ap())
    hymba_layer(nc, *args)
    r = run_bass_kernel_spmd(nc, [arrays], core_ids=[0])
    return r.results[0]["out_0_dram"]
```
